# Optimizing a Trainium2 kernel written in Bass

```python
import jax, jax.numpy as jnp
from jax import lax
import numpy as np

D_MODEL = 1024
BATCH = 1
SEQ = 1024
DEPTH = 1

GRID_W = 64
HEAD_DIM = 64
NA_HEADS = D_MODEL // 256
NA_WIDTH = NA_HEADS * HEAD_DIM
NA_KR_MAX = 8
NA_KC = 16
MLA_HEADS = D_MODEL // 128
MLA_NOPE = 64
MLA_ROPE = 32
MLA_V = 64
MLA_Q_RANK = 384
MLA_KV_RANK = 256
MLA_WIDTH = MLA_HEADS * MLA_V
ROPE_THETA = 10000.0
Q_BLOCK = 128
CONV_WIDTH = D_MODEL // 4
CONV_K = 3
D_MIX = NA_WIDTH + MLA_WIDTH + CONV_WIDTH
D_IN = 3 * NA_WIDTH + MLA_Q_RANK + MLA_KV_RANK + MLA_ROPE + 3 * CONV_WIDTH
OUT_GROUPS = D_MIX // HEAD_DIM
D_FF = -(-8 * D_MODEL // (3 * 256)) * 256
EPS = 1e-6


def rms_norm(x, g):
    xf = x.astype(jnp.float32)
    y = xf * lax.rsqrt(jnp.mean(xf * xf, axis=-1, keepdims=True) + EPS)
    return (y * g.astype(jnp.float32)).astype(x.dtype)

def ada_norm(x, g, shift, scale):
    return rms_norm(x, g) * (1 + scale) + shift

def rope_tables(positions):
    inv = ROPE_THETA ** (-jnp.arange(0, MLA_ROPE, 2, dtype=jnp.float32) / MLA_ROPE)
    ang = positions.astype(jnp.float32)[..., None] * inv
    return jnp.cos(ang), jnp.sin(ang)

def apply_rope(x, cos, sin):
    xf = x.astype(jnp.float32)
    x1, x2 = jnp.split(xf, 2, axis=-1)
    return jnp.concatenate([x1 * cos - x2 * sin, x2 * cos + x1 * sin], axis=-1).astype(x.dtype)

def neighbourhood_attention(q, k, v, rpb):
    b, t, h, dh = q.shape
    rows = t // GRID_W
    kr = min(NA_KR_MAX, rows)
    kc = NA_KC
    qg = q.reshape(b, rows, GRID_W, h, dh)
    kg = k.reshape(b, rows, GRID_W, h, dh)
    vg = v.reshape(b, rows, GRID_W, h, dh)
    r = jnp.arange(rows)
    row_start = jnp.clip(r - kr // 2, 0, rows - kr)
    row_idx = row_start[:, None] + jnp.arange(kr)[None, :]
    k_band = kg[:, row_idx]
    v_band = vg[:, row_idx]
    s = jnp.einsum('brqhd,brjwhd->bhrqjw', qg, k_band).astype(jnp.float32) * (dh ** -0.5)
    cols = jnp.arange(GRID_W)
    col_start = jnp.clip(cols - kc // 2, 0, GRID_W - kc)
    col_ok = (cols[None, :] >= col_start[:, None]) & (cols[None, :] < col_start[:, None] + kc)
    dr_i = row_idx - r[:, None] + NA_KR_MAX - 1
    dc_i = jnp.clip(cols[None, :] - cols[:, None] + kc - 1, 0, 2 * kc - 2)
    bias = rpb[:, dr_i[:, None, :, None], dc_i[None, :, None, :]]
    s = jnp.where(col_ok[:, None, :], s + bias.astype(jnp.float32)[None], -jnp.inf)
    p = jax.nn.softmax(s.reshape(b, h, rows, GRID_W, kr * GRID_W), axis=-1)
    p = p.reshape(s.shape).astype(v.dtype)
    o = jnp.einsum('bhrqjw,brjwhd->brqhd', p, v_band)
    return o.reshape(b, t, h * dh)

def latent_attention(c_q, c_kv, k_rope, q_a_g, kv_a_g, w_uq, w_ukv, qn_g, kn_g, qr_g, kr_g, cos, sin):
    b, t, _ = c_q.shape
    q = (rms_norm(c_q, q_a_g) @ w_uq).reshape(b, t, MLA_HEADS, MLA_NOPE + MLA_ROPE)
    kv = (rms_norm(c_kv, kv_a_g) @ w_ukv).reshape(b, t, MLA_HEADS, MLA_NOPE + MLA_V)
    q_nope = rms_norm(q[..., :MLA_NOPE], qn_g)
    q_rope = apply_rope(rms_norm(q[..., MLA_NOPE:], qr_g), cos[:, :, None], sin[:, :, None])
    k_nope = rms_norm(kv[..., :MLA_NOPE], kn_g)
    v = kv[..., MLA_NOPE:]
    k_r = apply_rope(rms_norm(k_rope, kr_g), cos, sin)
    scale = (MLA_NOPE + MLA_ROPE) ** -0.5
    nb = t // Q_BLOCK

    def to_blocks(a):
        return jnp.moveaxis(a.reshape(b, nb, Q_BLOCK, *a.shape[2:]), 1, 0)

    def block(qs):
        qn, qr = qs
        s = jnp.einsum('bqhd,bkhd->bhqk', qn, k_nope) + jnp.einsum('bqhr,bkr->bhqk', qr, k_r)
        p = jax.nn.softmax(s.astype(jnp.float32) * scale, axis=-1).astype(v.dtype)
        return jnp.einsum('bhqk,bkhd->bqhd', p, v)

    o = lax.map(block, (to_blocks(q_nope), to_blocks(q_rope)))
    return jnp.moveaxis(o, 0, 1).reshape(b, t, MLA_WIDTH)

def short_conv(x_in, gate_b, gate_c, conv_w, conv_b):
    u = gate_c * x_in
    y = lax.conv_general_dilated(u, conv_w[:, None, :], window_strides=(1,),
                                 padding=((CONV_K // 2, CONV_K // 2),),
                                 dimension_numbers=('NWC', 'WIO', 'NWC'),
                                 feature_group_count=CONV_WIDTH) + conv_b
    return gate_b * y

def first_inputs(seed: int = 0) -> dict:
    key = jax.random.key(seed)
    ks = jax.random.split(key, 24)
    f32 = jnp.float32

    def dense(k, shape, fan_in, mult=1.0):
        return jax.random.normal(k, shape, f32) * (mult * fan_in ** -0.5)

    def gain(k, shape):
        return 1.0 + 0.05 * jax.random.normal(k, shape, f32)

    def small(k, shape, s):
        return s * jax.random.normal(k, shape, f32)

    L = DEPTH
    return {
        'x': jax.random.normal(ks[0], (BATCH, SEQ, D_MODEL), f32),
        'c': jax.random.normal(ks[1], (BATCH, D_MODEL), f32),
        'positions': jnp.broadcast_to(jnp.arange(SEQ, dtype=jnp.int32), (BATCH, SEQ)),
        'norm1_g': gain(ks[2], (L, D_MODEL)),
        'norm2_g': gain(ks[3], (L, D_MODEL)),
        'w_ada': dense(ks[4], (L, D_MODEL, 6 * D_MODEL), D_MODEL, 0.5),
        'b_ada': small(ks[5], (L, 6 * D_MODEL), 0.02),
        'w_in': dense(ks[6], (L, D_MODEL, D_IN), D_MODEL),
        'na_q_g': gain(ks[7], (L, HEAD_DIM)),
        'na_k_g': gain(ks[8], (L, HEAD_DIM)),
        'na_rpb': small(ks[9], (L, NA_HEADS, 2 * NA_KR_MAX - 1, 2 * NA_KC - 1), 0.05),
        'mla_q_a_g': gain(ks[10], (L, MLA_Q_RANK)),
        'mla_kv_a_g': gain(ks[11], (L, MLA_KV_RANK)),
        'mla_w_uq': dense(ks[12], (L, MLA_Q_RANK, MLA_HEADS * (MLA_NOPE + MLA_ROPE)), MLA_Q_RANK),
        'mla_w_ukv': dense(ks[13], (L, MLA_KV_RANK, MLA_HEADS * (MLA_NOPE + MLA_V)), MLA_KV_RANK),
        'mla_qn_g': gain(ks[14], (L, MLA_NOPE)),
        'mla_kn_g': gain(ks[15], (L, MLA_NOPE)),
        'mla_qr_g': gain(ks[16], (L, MLA_ROPE)),
        'mla_kr_g': gain(ks[17], (L, MLA_ROPE)),
        'conv_w': dense(ks[18], (L, CONV_K, CONV_WIDTH), CONV_K),
        'conv_b': small(ks[19], (L, CONV_WIDTH), 0.02),
        'out_norm_g': gain(ks[20], (L, D_MIX)),
        'w_out': dense(ks[21], (L, D_MIX, D_MODEL), D_MIX),
        'w_gu': dense(ks[22], (L, D_MODEL, 2 * D_FF), D_MODEL),
        'w_down': dense(ks[23], (L, D_FF, D_MODEL), D_FF),
    }

def first_block(x, c, positions, norm1_g, norm2_g, w_ada, b_ada, w_in, na_q_g, na_k_g, na_rpb,
              mla_q_a_g, mla_kv_a_g, mla_w_uq, mla_w_ukv, mla_qn_g, mla_kn_g, mla_qr_g, mla_kr_g,
              conv_w, conv_b, out_norm_g, w_out, w_gu, w_down):
    b, t, _ = x.shape
    cos, sin = rope_tables(positions)
    c_act = jax.nn.silu(c)
    i0 = 3 * NA_WIDTH
    i1 = i0 + MLA_Q_RANK
    i2 = i1 + MLA_KV_RANK
    i3 = i2 + MLA_ROPE
    for l in range(DEPTH):
        mod = c_act @ w_ada[l] + b_ada[l]
        sh1, sc1, g1, sh2, sc2, g2 = jnp.split(mod[:, None, :], 6, axis=-1)
        h = ada_norm(x, norm1_g[l], sh1, sc1)
        proj = h @ w_in[l]
        na_qkv, c_q, c_kv, k_rope, conv_in = jnp.split(proj, [i0, i1, i2, i3], axis=-1)
        q, k, v = jnp.split(na_qkv, 3, axis=-1)
        q = rms_norm(q.reshape(b, t, NA_HEADS, HEAD_DIM), na_q_g[l])
        k = rms_norm(k.reshape(b, t, NA_HEADS, HEAD_DIM), na_k_g[l])
        v = v.reshape(b, t, NA_HEADS, HEAD_DIM)
        y_na = neighbourhood_attention(q, k, v, na_rpb[l])
        y_mla = latent_attention(c_q, c_kv, k_rope, mla_q_a_g[l], mla_kv_a_g[l], mla_w_uq[l],
                                 mla_w_ukv[l], mla_qn_g[l], mla_kn_g[l], mla_qr_g[l], mla_kr_g[l],
                                 cos, sin)
        x_in, gate_b, gate_c = jnp.split(conv_in, 3, axis=-1)
        y_conv = short_conv(x_in, gate_b, gate_c, conv_w[l], conv_b[l])
        mixed = jnp.concatenate([y_na, y_mla, y_conv], axis=-1)
        mixed = rms_norm(mixed.reshape(b, t, OUT_GROUPS, HEAD_DIM),
                         out_norm_g[l].reshape(OUT_GROUPS, HEAD_DIM)).reshape(b, t, D_MIX)
        x = x + g1 * (mixed @ w_out[l])
        h2 = ada_norm(x, norm2_g[l], sh2, sc2)
        gt, up = jnp.split(h2 @ w_gu[l], 2, axis=-1)
        x = x + g2 * ((jax.nn.silu(gt) * up) @ w_down[l])
    return x


DEPTH_2 = 2

N_A_LAYERS = DEPTH_2 // 2
N_B_LAYERS = DEPTH_2 - N_A_LAYERS

M_EXPAND = 2
M_D_INNER = M_EXPAND * D_MODEL
M_HEADDIM = 64
M_HEADS = M_D_INNER // M_HEADDIM
M_GROUPS = 4
M_D_STATE = 128
M_D_CONV = 4
M_CHUNK = 128
M_CONV_DIM = M_D_INNER + 2 * M_GROUPS * M_D_STATE
M_IN_DIM = 2 * M_D_INNER + 2 * M_GROUPS * M_D_STATE + M_HEADS

SB_HEAD_DIM = 64
SB_HEADS = D_MODEL // SB_HEAD_DIM
SB_WIDTH = SB_HEADS * SB_HEAD_DIM
SB_BLOCK = 128


def _rmsnorm(x, g):
    xf = x.astype(jnp.float32)
    xf = xf * lax.rsqrt(jnp.mean(xf * xf, axis=-1, keepdims=True) + EPS)
    return (xf * g.astype(jnp.float32)).astype(x.dtype)

def _modulate(x, g, shift, scale):
    return _rmsnorm(x, g) * (1.0 + scale[:, None, :]) + shift[:, None, :]

def _causal_dwconv(u, w, b):
    k = w.shape[0]
    out = lax.conv_general_dilated(
        u, w[:, None, :].astype(u.dtype), window_strides=(1,), padding=[(k - 1, 0)],
        dimension_numbers=('NWC', 'WIO', 'NWC'), feature_group_count=u.shape[-1])
    return out + b

def _ssd_chunked(xs, dt, a_neg, bm, cm):
    b, s, h, p = xs.shape
    g, n = bm.shape[2], bm.shape[3]
    hg = h // g
    nc = s // M_CHUNK
    xdt = (xs.astype(jnp.float32) * dt[..., None]).reshape(b, s, g, hg, p)
    a = (dt * a_neg).reshape(b, s, g, hg)

    def chunks(t):
        return jnp.moveaxis(t.reshape((b, nc, M_CHUNK) + t.shape[2:]), 1, 0)

    causal = jnp.tril(jnp.ones((M_CHUNK, M_CHUNK), dtype=bool))[None, :, :, None, None]

    def step(state, inp):
        xc, ac, bc, cc = inp
        acum = jnp.cumsum(ac, axis=1)
        seg = jnp.where(causal, acum[:, :, None] - acum[:, None, :], -jnp.inf)
        scores = jnp.einsum('btgn,bsgn->btsg', cc, bc)[..., None] * jnp.exp(seg)
        y_diag = jnp.einsum('btsgh,bsghp->btghp', scores, xc)
        y_off = jnp.einsum('btgn,bghpn->btghp', cc, state) * jnp.exp(acum)[..., None]
        w_end = jnp.exp(acum[:, -1:] - acum)
        new_state = (state * jnp.exp(acum[:, -1])[..., None, None]
                     + jnp.einsum('bsgn,bsghp->bghpn', bc, xc * w_end[..., None]))
        return new_state, y_diag + y_off

    state0 = jnp.zeros((b, g, hg, p, n), jnp.float32)
    _, ys = lax.scan(step, state0, (chunks(xdt), chunks(a),
                                    chunks(bm.astype(jnp.float32)), chunks(cm.astype(jnp.float32))))
    return jnp.moveaxis(ys, 0, 1).reshape(b, s, h, p)

def _mamba2_mixer(h, in_w, conv_w, conv_b, dt_bias, a_log, d_skip, norm_g, out_w):
    b, s, _ = h.shape
    zxbcdt = h @ in_w
    z = zxbcdt[..., :M_D_INNER]
    xbc = zxbcdt[..., M_D_INNER:M_D_INNER + M_CONV_DIM]
    dt = zxbcdt[..., M_D_INNER + M_CONV_DIM:]
    xbc = jax.nn.silu(_causal_dwconv(xbc, conv_w, conv_b))
    gn = M_GROUPS * M_D_STATE
    xs = xbc[..., :M_D_INNER].reshape(b, s, M_HEADS, M_HEADDIM)
    bm = xbc[..., M_D_INNER:M_D_INNER + gn].reshape(b, s, M_GROUPS, M_D_STATE)
    cm = xbc[..., M_D_INNER + gn:].reshape(b, s, M_GROUPS, M_D_STATE)
    dt = jax.nn.softplus(dt.astype(jnp.float32) + dt_bias.astype(jnp.float32))
    a_neg = -jnp.exp(a_log.astype(jnp.float32))
    y = _ssd_chunked(xs, dt, a_neg, bm, cm)
    y = y + d_skip.astype(jnp.float32)[:, None] * xs.astype(jnp.float32)
    y = y.reshape(b, s, M_D_INNER) * jax.nn.silu(z.astype(jnp.float32))
    yg = y.reshape(b, s, M_GROUPS, M_D_INNER // M_GROUPS)
    yg = yg * lax.rsqrt(jnp.mean(yg * yg, axis=-1, keepdims=True) + EPS)
    y = yg.reshape(b, s, M_D_INNER) * norm_g.astype(jnp.float32)
    return y.astype(h.dtype) @ out_w

def _stick_breaking(q, k, v):
    s_len = q.shape[1]
    scale = SB_HEAD_DIM ** -0.5
    outs = []
    for i in range(s_len // SB_BLOCK):
        lo, hi = i * SB_BLOCK, (i + 1) * SB_BLOCK
        z = jnp.einsum('bthd,bshd->bhts', q[:, lo:hi], k[:, :hi]).astype(jnp.float32) * scale
        mask = ((lo + jnp.arange(SB_BLOCK))[:, None] > jnp.arange(hi)[None, :])[None, None]
        log_keep = jnp.where(mask, jax.nn.log_sigmoid(-z), 0.0)
        after = lax.cumsum(log_keep, axis=3, reverse=True) - log_keep
        log_a = jnp.where(mask, jax.nn.log_sigmoid(z) + after, -jnp.inf)
        a = jnp.exp(log_a).astype(v.dtype)
        outs.append(jnp.einsum('bhts,bshd->bthd', a, v[:, :hi]))
    return jnp.concatenate(outs, axis=1)

def _sb_mixer(h, k, v, in_w, out_w):
    b, s, _ = h.shape
    qz = h @ in_w
    q = qz[..., :SB_WIDTH].reshape(b, s, SB_HEADS, SB_HEAD_DIM)
    z = qz[..., SB_WIDTH:]
    o = _stick_breaking(q, k, v).reshape(b, s, SB_WIDTH)
    return (o * jax.nn.silu(z)) @ out_w

def second_inputs(seed: int = 0) -> dict:
    key = jax.random.key(seed)
    ks = jax.random.split(key, 24)
    f32 = jnp.float32

    def nrm(k, shape, fan_in, mult=1.0):
        return jax.random.normal(k, shape, f32) * (mult * fan_in ** -0.5)

    def gain(k, shape):
        return 1.0 + 0.05 * jax.random.normal(k, shape, f32)

    def small(k, shape):
        return 0.01 * jax.random.normal(k, shape, f32)

    x = jax.random.normal(ks[0], (BATCH, SEQ, D_MODEL), f32)
    c = jax.random.normal(ks[1], (BATCH, D_MODEL), f32)
    ada_w = nrm(ks[2], (DEPTH_2, D_MODEL, 3 * D_MODEL), D_MODEL, 0.5)
    ada_b = small(ks[3], (DEPTH_2, 3 * D_MODEL))
    norm_g = gain(ks[4], (DEPTH_2, D_MODEL))
    m_in_w = nrm(ks[5], (N_A_LAYERS, D_MODEL, M_IN_DIM), D_MODEL)
    m_conv_w = nrm(ks[6], (N_A_LAYERS, M_D_CONV, M_CONV_DIM), M_D_CONV)
    m_conv_b = small(ks[7], (N_A_LAYERS, M_CONV_DIM))
    dt0 = jnp.exp(jax.random.uniform(ks[8], (N_A_LAYERS, M_HEADS), f32,
                                     np.log(1e-3).astype(np.float32), np.log(1e-1).astype(np.float32)))
    m_dt_bias = dt0 + jnp.log(-jnp.expm1(-dt0))
    m_a_log = jnp.log(jax.random.uniform(ks[9], (N_A_LAYERS, M_HEADS), f32, 1.0, 16.0))
    m_d = 1.0 + 0.1 * jax.random.normal(ks[10], (N_A_LAYERS, M_HEADS), f32)
    m_norm_g = gain(ks[11], (N_A_LAYERS, M_D_INNER))
    m_out_w = nrm(ks[12], (N_A_LAYERS, M_D_INNER, D_MODEL), M_D_INNER)
    kv_ada_w = nrm(ks[13], (D_MODEL, 2 * D_MODEL), D_MODEL, 0.5)
    kv_ada_b = small(ks[14], (2 * D_MODEL,))
    kv_norm_g = gain(ks[15], (D_MODEL,))
    kv_w = nrm(ks[16], (D_MODEL, 2 * SB_WIDTH), D_MODEL)
    sb_in_w = nrm(ks[17], (N_B_LAYERS, D_MODEL, 2 * SB_WIDTH), D_MODEL)
    sb_out_w = nrm(ks[18], (N_B_LAYERS, SB_WIDTH, D_MODEL), SB_WIDTH)
    final_g = gain(ks[19], (D_MODEL,))
    return {'x': x, 'c': c, 'ada_w': ada_w, 'ada_b': ada_b, 'norm_g': norm_g,
            'm_in_w': m_in_w, 'm_conv_w': m_conv_w, 'm_conv_b': m_conv_b,
            'm_dt_bias': m_dt_bias, 'm_a_log': m_a_log, 'm_d': m_d,
            'm_norm_g': m_norm_g, 'm_out_w': m_out_w,
            'kv_ada_w': kv_ada_w, 'kv_ada_b': kv_ada_b, 'kv_norm_g': kv_norm_g, 'kv_w': kv_w,
            'sb_in_w': sb_in_w, 'sb_out_w': sb_out_w, 'final_g': final_g}

def second_block(x, c, ada_w, ada_b, norm_g, m_in_w, m_conv_w, m_conv_b, m_dt_bias, m_a_log,
              m_d, m_norm_g, m_out_w, kv_ada_w, kv_ada_b, kv_norm_g, kv_w,
              sb_in_w, sb_out_w, final_g):
    b, s, _ = x.shape
    c_act = jax.nn.silu(c)

    for i in range(N_A_LAYERS):
        shift, scale, gate = jnp.split(c_act @ ada_w[i] + ada_b[i], 3, axis=-1)
        h = _modulate(x, norm_g[i], shift, scale)
        y = _mamba2_mixer(h, m_in_w[i], m_conv_w[i], m_conv_b[i], m_dt_bias[i], m_a_log[i],
                          m_d[i], m_norm_g[i], m_out_w[i])
        x = x + gate[:, None, :] * y

    kv_shift, kv_scale = jnp.split(c_act @ kv_ada_w + kv_ada_b, 2, axis=-1)
    hk = _modulate(x, kv_norm_g, kv_shift, kv_scale)
    kv = hk @ kv_w
    k = kv[..., :SB_WIDTH].reshape(b, s, SB_HEADS, SB_HEAD_DIM)
    v = kv[..., SB_WIDTH:].reshape(b, s, SB_HEADS, SB_HEAD_DIM)

    for j in range(N_B_LAYERS):
        i = N_A_LAYERS + j
        shift, scale, gate = jnp.split(c_act @ ada_w[i] + ada_b[i], 3, axis=-1)
        h = _modulate(x, norm_g[i], shift, scale)
        y = _sb_mixer(h, k, v, sb_in_w[j], sb_out_w[j])
        x = x + gate[:, None, :] * y

    return _rmsnorm(x, final_g)


def setup_inputs(seed=0):
    out = dict(first_inputs(seed))
    for name, value in second_inputs(seed + 1).items():
        if name != "x":
            out[name + "_2"] = value
    return out


def reference(
    x, c, positions, norm1_g, norm2_g, w_ada, b_ada, w_in, na_q_g, na_k_g, na_rpb, mla_q_a_g,
    mla_kv_a_g, mla_w_uq, mla_w_ukv, mla_qn_g, mla_kn_g, mla_qr_g, mla_kr_g, conv_w, conv_b,
    out_norm_g, w_out, w_gu, w_down, c_2, ada_w_2, ada_b_2, norm_g_2, m_in_w_2, m_conv_w_2,
    m_conv_b_2, m_dt_bias_2, m_a_log_2, m_d_2, m_norm_g_2, m_out_w_2, kv_ada_w_2, kv_ada_b_2,
    kv_norm_g_2, kv_w_2, sb_in_w_2, sb_out_w_2, final_g_2,
):
    x = first_block(
        x, c, positions, norm1_g, norm2_g, w_ada, b_ada, w_in, na_q_g, na_k_g, na_rpb,
        mla_q_a_g, mla_kv_a_g, mla_w_uq, mla_w_ukv, mla_qn_g, mla_kn_g, mla_qr_g, mla_kr_g,
        conv_w, conv_b, out_norm_g, w_out, w_gu, w_down,
    )
    return second_block(
        x, c_2, ada_w_2, ada_b_2, norm_g_2, m_in_w_2, m_conv_w_2, m_conv_b_2, m_dt_bias_2,
        m_a_log_2, m_d_2, m_norm_g_2, m_out_w_2, kv_ada_w_2, kv_ada_b_2, kv_norm_g_2, kv_w_2,
        sb_in_w_2, sb_out_w_2, final_g_2,
    )


_drawn_inputs = setup_inputs


def setup_inputs(seed=0):
    import zlib

    import numpy as np

    out = dict(_drawn_inputs(seed))
    spreads = {}
    factors = {'norm1_g': 3.527,
     'norm2_g': 3.863,
     'na_q_g': 8.0,
     'na_k_g': 8.0,
     'na_rpb': 8.0,
     'mla_q_a_g': 8.0,
     'mla_kv_a_g': 4.67,
     'mla_qn_g': 8.0,
     'mla_kn_g': 8.0,
     'mla_qr_g': 8.0,
     'mla_kr_g': 8.0,
     'conv_b': 47.909,
     'out_norm_g': 3.783,
     'ada_b_2': 4.724,
     'm_conv_b_2': 8.0,
     'm_d_2': 3.784,
     'm_norm_g_2': 11.761,
     'kv_ada_b_2': 8.0,
     'kv_norm_g_2': 8.0}
    for name, (base, spread) in spreads.items():
        noise = np.random.default_rng([zlib.crc32(name.encode()), seed]).standard_normal(out[name].shape)
        drawn = base * np.exp(spread * noise) if base else spread * noise
        out[name] = __import__('jax').numpy.asarray(drawn.astype(out[name].dtype))
    for name, factor in factors.items():
        out[name] = (out[name] * factor).astype(out[name].dtype)
    return out
```

```python
from contextlib import ExitStack, contextmanager

import numpy as np

import concourse.bass as bass
from concourse import mybir

F32 = mybir.dt.float32
F32R = mybir.dt.float32r
I32 = mybir.dt.int32
ALU = mybir.AluOpType
ACT = mybir.ActivationFunctionType
AX = mybir.AxisListType

P = 128
D = 1024
T = 1024
KD = D // P
TT = T // P
HD = 64
NAH = 4
MH = 8
QR, KVR, ROPE = 384, 256, 32
CW = 256
DFF = 2816
FT = DFF // P
GRID = 64
KR, KC = 8, 16
EPS = 1e-6
NEG = -1e30
DI = 2048
NH = 32
NG = 4
DS = 128
SBH = 16
MROWS = 2 * D
PI = float(np.pi)


class Cursor:

    def __init__(self):
        self.n = 0
        self.i = None
        self.per = 0

    def at(self, k=0):
        n = self.n + k
        m = n // 2
        if self.i is not None:
            m = m + self.i * (self.per // 2)
        return n % 2, m

    def enter(self, i, per):
        self.i, self.per, self.start = i, per, self.n

    def leave(self, times):
        assert self.n - self.start == self.per and self.per % 2 == 0, (self.n - self.start, self.per)
        self.n = self.start + self.per * times
        self.i = None


class Tally:

    def __init__(self, n=0):
        self.n = n
        self.i = None
        self.per = 0

    def __call__(self, k=0):
        v = self.n + k
        return v if self.i is None else v + self.i * self.per

    def next(self, k=1):
        self.n += k
        return self()

    def enter(self, i, per):
        self.i, self.per, self.start = i, per, self.n

    def leave(self, times):
        assert self.n - self.start == self.per, (self.n - self.start, self.per)
        self.n = self.start + self.per * times
        self.i = None


@contextmanager
def counted(eng, times, counters):
    with eng.Fori(0, times) as i:
        for c, per in counters:
            c.enter(i, per)
        yield i
    for c, _ in counters:
        c.leave(times)


VEC = {}


def _vec(name, n):
    VEC[name] = (_vec.at, n)
    _vec.at += n


_vec.at = 0
for _name, _n in (("norm1_g", 8), ("norm2_g", 8), ("b_ada", 48), ("conv_w", 6), ("conv_b", 2),
                  ("q_a_g", 3), ("kv_a_g", 2), ("na_q_g", 1), ("na_k_g", 1), ("mla_q_g", 1),
                  ("mla_k_g", 1), ("out_norm_g", 8)):
    _vec(_name, _n)
_vec.at = 128
for _name, _n in (("ada_b_2", 48), ("kv_ada_b_2", 16), ("norm_g_2", 16), ("m_conv_b_2", 24),
                  ("dt_bias", 1), ("a_log", 1), ("kv_norm_g_2", 8), ("final_g_2", 8)):
    _vec(_name, _n)
_vec.at = 256
for _name, _n in (("m_conv_w_2", 96), ("m_norm_g_2", 16), ("c", 8), ("c_2", 8)):
    _vec(_name, _n)
NVEC = 3
TWO_PI = (6.28125, 0.0019350051879882812, 3.019915981956753e-07)

MOD = {"sh1": 0, "sc1": 8, "g1": 16, "sh2": 24, "sc2": 32, "g2": 40,
       "m_sh": 48, "m_sc": 56, "m_g": 64, "s_sh": 72, "s_sc": 80, "s_g": 88, "kv_sh": 96, "kv_sc": 104}
Q0 = 0
K0 = NAH * HD
V0 = 2 * NAH * HD
CQ0 = 3 * NAH * HD
CKV0 = CQ0 + QR
KROPE0 = CKV0 + KVR
XIN0 = KROPE0 + ROPE
GB0 = XIN0 + CW
GC0 = GB0 + CW
WIN_UNITS = ([("x", 0, XIN0), ("gc", 0, GC0), ("gb", 0, GB0), ("x", 1, XIN0 + P), ("gc", 1, GC0 + P), ("gb", 1, GB0 + P)]
             + [("q", t, Q0 + t * P) for t in range(2)] + [("k", t, K0 + t * P) for t in range(2)]
             + [("v", t, V0 + t * P) for t in range(2)] + [("cq", t, CQ0 + t * P) for t in range(3)]
             + [("ckv", t, CKV0 + t * P) for t in range(2)] + [("krope", 0, KROPE0)])
ADA_AT_UNIT = [2] * 6 + [1] * 4 + [2] * 8
NARROW = (len(WIN_UNITS) - 1, len(WIN_UNITS) + KD + 6 * (FT // 2))
KV_UNIT0 = len(WIN_UNITS) + 2 * MH + TT // 2 + 6 + KD + 4 * (FT // 2) + KD * (FT // 2) + 1 + 22 * NG
OUT_UNIT0 = KV_UNIT0 + 4 * KD + KD
X0 = DI
B0 = X0 + DI
C0 = B0 + NG * DS
DT0 = C0 + NG * DS
ADA_COLUMNS = 2 * KD
NA_PAIRS = [(0, 7), (0, 5), (0, 3), (2, 3), (4, 3), (6, 3), (8, 3), (8, 1)]


def two_blocks(nc, a, out):
    scr_bias = nc.dram_tensor("bias_rows", (NAH * (2 * KR - 1), GRID, P), F32, kind="Internal").ap()
    scr_heads = [nc.dram_tensor(f"heads_{n}", (KD, P, T), F32, kind="Internal").ap() for n in ("k", "v", "q", "z")]
    ctx = ExitStack()
    with ctx:
        base = -(-nc.sbuf_base // 32) * 32

        def at(name, off, shape, dt=F32):
            n = int(np.prod(shape[1:]))
            assert off + n <= 53000, name
            return nc.alloc_sbuf_tensor_at(name, list(shape), dt, offset=base + 4 * off)

        def sem(name):
            return ctx.enter_context(nc.semaphore(name))

        xT = at("xT", 0, [P, KD, T])
        w_raw = at("w_raw", 8192, [P, 2, 1024])
        w_hi_t = at("w_hi_t", 10240, [P, 2, 1024], F32R)
        w_lo_t = at("w_lo_t", 12288, [P, 2, 1024], F32R)
        ada_w = at("ada_w", 14336, [P, 2, KD, P])
        C = 16384
        ada_acc = at("ada_acc", C, [P, 2, P])
        ident = at("ident", C + 256, [P, P])
        ones = at("ones", C + 384, [P, P])
        blk64 = at("blk64", C + 512, [P, P])
        blk96 = at("blk96", C + 640, [P, P])
        tri = at("tri", C + 768, [P, P])
        vec = at("vec", C + 896, [P, NVEC * P])
        mod = at("mod", C + 1280, [P, 112])
        coef = at("coef", C + 1392, [P, 5, 8])
        small = at("small", C + 1432, [P, 64])
        cact = at("cact", C + 1496, [P, 16])
        kv_row = at("kv_row", C + 1512, [P, 16])
        inv3 = at("inv3", 15360, [P, TT, 96])
        na_mask = at("na_mask", C + 1576, [P, GRID])
        rt = at("rt", C + 1528, [P, 2, 3 * TT])
        H = 18432
        hH = at("hH", H, [P, KD, T], F32R)
        hL = at("hL", H + 8192, [P, KD, T], F32R)
        A = 34816
        x_stage = at("x_stage", A, [P, TT, D])
        v_stage = at("v_stage", A + 8192, [P, NVEC, P])
        n_sq = at("n_sq", A + 14336, [P, 2, T])
        n_rs = at("n_rs", A + 11264, [P, T])
        n_x = at("n_x", A + 12288, [P, 2, T])
        n_h = at("n_h", A + 14336, [P, 2, T])
        rp = at("rp", A + 16384, [P, P])
        conv_u = at("conv_u", A, [P, T + 2])
        conv_x = at("conv_x", A + 1032, [P, T])
        conv_v = at("conv_v", A + 2056, [P, T])
        na_q = at("na_q", A, [P, 2, T])
        na_k = at("na_k", A + 2048, [P, 2, T])
        y_na = at("y_na", A + 4096, [P, TT, 256])
        na_v = at("na_v", A + 6144, [P, TT, 256])
        j_sq = at("j_sq", A + 8192, [P, T])
        j_rs = at("j_rs", A + 9216, [P, T])
        y_conv = at("y_conv", A + 10496, [P, 2, T])
        cq = at("cq", A + 12544, [P, 3, T])
        ckv = at("ckv", A + 15616, [P, 2, T])
        b2 = at("b2", H, [P, NAH, 16, GRID])
        bint = at("bint", H + 4096, [P, NAH, 9, GRID])
        na_p = at("na_p", H + 6400, [P, 2, 576])
        na_pt = at("na_pt", H + 7552, [P, 2, 5, P])
        na_ks = at("na_ks", H + 8832, [HD, 2, T])
        na_qs = at("na_qs", H + 10880, [HD, 2, T])
        mq = at("mq", H, [P, MH, T])
        mk = at("mk", H + 8192, [P, MH, T])
        rope = at("rope", A, [P, 2, T])
        rope_t = at("rope_t", A + 2048, [P, T])
        rope_k = at("rope_k", A + 3072, [P, T])
        k_raw = at("k_raw", H + 13312, [P, T])
        mv = at("mv", A, [P, TT, MH * HD])
        wuq = at("wuq", A + 6144, [P, 3, 768])
        wukv = at("wukv", A + 8448, [P, 2, 1024])
        u_sq = at("u_sq", 14336, [P, T])
        u_rs = at("u_rs", 15360, [P, T])
        y_mla = at("y_mla", A + 6144, [P, TT, 512])
        m_p = at("m_p", A + 12544, [P, 2, T])
        m_pt = at("m_pt", A + 14592, [P, 2, TT, P])
        m_qs = at("m_qs", A + 16640, [P, 2, P])
        g_h = at("g_h", A, [P, 2, T])
        g_t = at("g_t", A + 2048, [P, 2, T])
        g_sq = at("g_sq", A + 12544, [P, 4096])
        g_rs = at("g_rs", A + 16640, [P, 96])
        f_silu = at("f_silu", A, [P, 2, T])
        f_prod = at("f_prod", A + 2048, [P, 2, T])
        f_hi = at("f_hi", A + 4096, [P, 2, T], F32R)
        f_lo = at("f_lo", A + 6144, [P, 2, T], F32R)

        zt = at("zt", A, [P, TT, 512])
        xt = at("xt", A + 4096, [P, TT, 512])
        bt = at("bt", A + 8192, [P, TT, DS])
        bT = at("bT", A + 9216, [P, T])
        cT = at("cT", A + 10240, [P, T])
        c_raw = at("c_raw", A + 11264, [P, 2, 1032])
        c_out = at("c_out", A + 13328, [P, 2, T])
        seg = at("seg", A + 11264, [P, 2, 8, P])
        xdt = at("xdt", A + 13312, [P, 2, 512])
        xw = at("xw", A + 14336, [P, 2, 512])
        state = at("state", A + 15376, [P, 2, 512])
        y1 = at("y1", 15872, [P, 512])
        xd = at("xd", A + 16400, [P, 2, 512])
        cbm = at("cbm", A + 17424, [P, 2, P])
        pool_t = at("pool_t", A + 17888, [P, 3, 64])
        tril = at("tril", A + 17416, [P, P])
        later = at("later", A + 16392, [P, T])
        d_row = at("d_row", A + 17680, [P, NH])
        m_ss = at("m_ss", A + 17712, [P, 8])
        ag = at("ag", A + 17720, [P, TT, 8])
        acg = at("acg", A + 17784, [P, TT, 8])
        cg_w = at("cg_w", A + 17848, [P, 4, 6])
        cg_b = at("cg_b", A + 17872, [P, 8])
        ng = at("ng", A + 17880, [P, 8])
        y_hi = at("y_hi", A + 4096, [P, 4, T], F32R)
        y_lo = at("y_lo", A + 8192, [P, 4, T], F32R)
        y_t32 = at("y_t32", A + 12288, [P, 2, T])
        dt_w = at("dt_w", A, [NH, 4, T])
        dt_t = at("dt_t", 14336, [P, TT, NH])
        a_t = at("a_t", 14592, [P, TT, NH])
        acum = at("acum", 14848, [P, TT, NH])
        eacum = at("eacum", 15104, [P, TT, NH])
        wend = at("wend", 15360, [P, TT, NH])
        etot = at("etot", 15616, [P, TT, NH])
        stage = at("stage", A, [P, 4, T])
        s_k = at("s_k", A, [P, 2, T])
        s_v = at("s_v", A + 2048, [P, 2, TT, P])
        s_q = at("s_q", A + 4096, [P, 2, T])
        s_z = at("s_z", A + 6144, [P, 2, T])
        v_f = at("v_f", A + 8192, [P, T])
        s_sig = at("s_sig", A + 8192, [P, 3, T])
        s_keep = at("s_keep", A + 12288, [P, 2, T])
        s_prod = at("s_prod", A + 11264, [P, T])
        s_at = at("s_at", A + 14336, [P, 2, TT, P])
        s_of = at("s_of", 14336, [P, 2, T])
        f_out = at("f_out", A, [P, TT, D])

        PU = ctx.enter_context(nc.psum_tensor("PU", [P, 2, 2, 512], F32))
        PM = ctx.enter_context(nc.psum_tensor("PM", [P, 4, 512], F32))

        def unit_ps(p, rows=P, r0=0):
            return PU[r0:r0 + rows, p, :, :].rearrange("p a b -> p (a b)")

        stat_ps = PM[:, 0:2, :].rearrange("p a b -> p (a b)")

        def v(name, k=0, n=1, rows=P, r0=0):
            c = VEC[name][0] + k
            return vec[r0:r0 + rows, c:c + n]

        def m(name, k=0, n=1):
            return mod[:, MOD[name] + k:MOD[name] + k + n]

        w_landed = [sem("w_landed0"), sem("w_landed1")]
        w_hi = [sem("w_hi0"), sem("w_hi1")]
        w_split = [sem("w_split0"), sem("w_split1")]
        unit_done = [sem("unit_done0"), sem("unit_done1")]
        unit_free = [sem("unit_free0"), sem("unit_free1")]
        ada_landed = [sem("ada_landed0"), sem("ada_landed1")]
        ada_acc_s = sem("ada_accumulated")
        ada_col = sem("ada_column_in_psum")
        ada_mod = sem("ada_modulation_written")
        vec_dma = sem("vec_rows_landed")
        vec_zero = sem("vec_stage_zeroed")
        vec_t = sem("vec_transposed")
        vec_done = sem("vec_table_ready")
        cact_done = sem("silu_c_ready")
        x_landed = [sem(f"x_landed{t}") for t in range(TT)]
        x_t = sem("x_tile_transposed")
        x_ev = [sem("x_evacuated_even"), sem("x_evacuated_odd")]
        consts = sem("constants_ready")
        pchain = sem("pool_steps")
        achain = sem("scalar_steps")
        vchain = sem("vector_steps")
        sq_ready = sem("squares_ready")
        stat_done = sem("sum_of_squares_done")
        std_ready = sem("root_ready")
        h_tmp = sem("h_float32_ready")
        h_hi = sem("h_high_ready")
        h_ready = sem("h_tile_ready")
        rope_dma = sem("positions_landed")
        rope_f = sem("rope_frequencies_landed")
        rope_arg = sem("rope_angles_reduced")
        rope_done = sem("rope_tables_ready")
        j_done = sem("head_norm_applied")
        rp_zero = sem("rpb_stage_zeroed")
        rp_landed = sem("rpb_landed")
        rp_spread = sem("rpb_rows_in_dram")
        b2_landed = sem("bias_tables_landed")
        na_stage = sem("na_head_staged")
        na_kstage = sem("na_keys_staged")
        na_s = sem("na_scores_done")
        na_l = sem("na_logits_ready")
        na_e = sem("na_exp_done")
        na_tr = sem("na_probs_transposed")
        na_ev = sem("na_probs_evacuated")
        na_pv = sem("na_values_summed")
        na_o = sem("na_output_written")
        wu_landed = sem("w_uq_w_ukv_landed")
        mh_done = sem("mla_head_rows_ready")
        rope_x = sem("rope_rows_ready")
        y_sq = sem("mixer_squares_ready")
        y_sum = sem("mixer_sums_ready")
        y_root = sem("mixer_roots_ready")
        mla_q = sem("mla_query_staged")
        mla_s = sem("mla_scores_done")
        mla_m = sem("mla_maximum_ready")
        mla_e = sem("mla_exp_done")
        mla_tr = sem("mla_probs_transposed")
        mla_ev = sem("mla_probs_evacuated")
        mla_pv = sem("mla_values_summed")
        mla_o = sem("mla_output_written")
        y_norm = sem("mixer_rows_normalised")
        f_hi_s = sem("gated_product_high_ready")
        f_act = sem("gated_product_split")

        c_sum = sem("head_squares_summed")
        c_root = sem("root_columns_ready")
        c_inv = sem("inverse_columns_ready")
        c_bc = sem("inverse_roots_spread")
        h_app = sem("mla_head_normalised")
        dt_x = sem("dt_exponential_ready")
        dt_f = sem("dt_feature_major_ready")
        dt_t_s = sem("dt_transposed")
        dt_tok = sem("dt_token_major")
        dt_sum = sem("dt_decays_summed")
        dt_log = sem("dt_log_decays_ready")
        dt_exp = sem("dt_decays_ready")
        dt_done = sem("dt_tables_ready")
        d_landed = sem("d_skip_landed")
        cv_done = sem("conv_done")
        cv_act = sem("conv_activated")
        cv_tr = sem("conv_tile_transposed")
        cv_tok = sem("conv_tile_token_major")
        ag_done = sem("group_tables_staged")
        ss_bc = sem("ssd_decays_broadcast")
        ss_seg = sem("ssd_segments_ready")
        ss_exp = sem("ssd_segments_exponentiated")
        ss_m = sem("ssd_scores_ready")
        ss_cbr = sem("ssd_cb_read")
        ss_x = sem("ssd_x_scaled")
        ss_off = sem("ssd_state_output_done")
        ss_y = sem("ssd_diagonal_output_done")
        ss_s = sem("ssd_state_update_done")
        ss_st = sem("ssd_state_written")
        ss_g = sem("ssd_output_gated")
        ss_sq = sem("ssd_output_squared")
        m_root = sem("group_root_ready")
        m_norm = sem("group_normalised")
        y_hi_s = sem("group_tile_high")
        y_lo_s = sem("group_tile_low")
        st_done = [sem(f"heads_stored{k}") for k in range(4)]
        sl_landed = [sem("pair_landed0"), sem("pair_landed1")]
        s_s = sem("sb_scores_done")
        s_sg = sem("sb_sigmoids_ready")
        s_mk = sem("sb_diagonal_masked")
        s_a = sem("sb_weights_ready")
        s_tr = sem("sb_weights_transposed")
        s_ev = [sem("sb_weights_evacuated_even"), sem("sb_weights_evacuated_odd")]
        s_pv = sem("sb_values_summed")
        s_o = sem("sb_output_gated")
        ep_hi = sem("sb_pair_high")
        ep_lo = sem("sb_pair_low")
        v_tr = sem("values_transposed")
        v_ev = sem("values_staged")
        o_mask = sem("mask_space_free")
        o_xn = sem("final_rows_scaled")
        o_st = [sem("out_stored0"), sem("out_stored1")]

        block = ctx.enter_context(nc.Block())

        @block.sync
        def _(sp):
            pc = Cursor()
            x_v = a["x"].rearrange("o (t p) d -> p (o t) d", p=P)
            for t in range(TT):
                sp.dma_start(x_stage[:, t, :], x_v[:, t, :]).then_inc(x_landed[t], 16)

            def panel(src, kt, width):
                p, n = pc.at()
                if pc.n >= 2:
                    sp.wait_ge(w_split[p], n)
                if callable(src):
                    src = src()
                dst = w_raw[:, p, 0:kt * width].rearrange("p (k c) -> p k c", k=kt)
                sp.dma_start(dst, src).then_inc(w_landed[p], 16)
                pc.n += 1

            w_in = a["w_in"].rearrange("o (k p) c -> p (o k) c", p=P)
            for kind, t, c0 in WIN_UNITS:
                panel(w_in[:, :, c0:c0 + (ROPE if kind == "krope" else P)], KD, ROPE if kind == "krope" else P)
            w_out = a["w_out"].rearrange("o (k p) c -> p (o k) c", p=P)
            for t in range(KD):
                panel(w_out[:, :, t * P:(t + 1) * P], KD, P)
            w_gu = a["w_gu"].rearrange("o (k p) c -> p (o k) c", p=P)
            w_dn = a["w_down"].rearrange("o (k p) c -> p (o k) c", p=P)

            def gate_up(i, t, up):
                panel(w_gu[:, :, bass.ds((2 * i + t) * P + up * DFF, P)], KD, P)

            def down(i):
                for c in range(2):
                    panel(w_dn[:, bass.ds(2 * i, 2), c * 512:(c + 1) * 512], 2, 512)

            for t, up in ((0, 0), (0, 1), (1, 0), (1, 1)):
                gate_up(0, t, up)
            with sp.Fori(0, FT // 2 - 1) as i:
                pc.enter(i, 6)
                gate_up(i + 1, 0, 0)
                gate_up(i + 1, 0, 1)
                gate_up(i + 1, 1, 0)
                down(i)
                gate_up(i + 1, 1, 1)
            pc.leave(FT // 2 - 1)
            down(FT // 2 - 1)

            m_in = a["m_in_w_2"].rearrange("o (k p) c -> p (o k) c", p=P)
            m_out = a["m_out_w_2"].rearrange("o (k p) c -> p (o k) c", p=P)
            panel(m_in[:, :, DT0:DT0 + NH], KD, NH)
            with counted(sp, NG, [(pc, 14)]) as i:
                for j in range(4):
                    panel(m_in[:, :, bass.ds(X0 + (4 * i + j) * P, P)], KD, P)
                panel(m_in[:, :, bass.ds(B0 + i * P, P)], KD, P)
                panel(m_in[:, :, bass.ds(C0 + i * P, P)], KD, P)
                for j in range(4):
                    panel(lambda: m_in[:, :, bass.ds(i * (4 * P) + j * P, P)], KD, P)
                for c in range(4):
                    panel(m_out[:, bass.ds(4 * i, 4), c * 256:(c + 1) * 256], 4, 256)
            kvw = a["kv_w_2"].rearrange("(k p) c -> p k c", p=P)
            sbw = a["sb_in_w_2"].rearrange("o (k p) c -> p (o k) c", p=P)
            with counted(sp, KD, [(pc, 2)]) as i:
                panel(lambda: kvw[:, :, bass.ds(D + i * P, P)], KD, P)
                panel(lambda: kvw[:, :, bass.ds(i * 2 * (P // 2), P)], KD, P)
            with counted(sp, KD, [(pc, 2)]) as i:
                panel(lambda: sbw[:, :, bass.ds(i * P, P)], KD, P)
                panel(lambda: sbw[:, :, bass.ds(D + i * P, P)], KD, P)
            s_out = a["sb_out_w_2"].rearrange("o (k p) c -> p (o k) c", p=P)
            for t in range(2):
                panel(s_out[:, :, t * P:(t + 1) * P], KD, P)
            for k in range(4):
                sp.wait_ge(st_done[k], 16 * KD)

            def pair_load(b, pair):
                for k, dst in enumerate((s_k[:, b, :], s_v[:, b, :, :].rearrange("p a c -> p (a c)"),
                                         s_q[:, b, :], s_z[:, b, :])):
                    sp.dma_start(dst, scr_heads[k][bass.ds(pair, 1), :, :].rearrange("o p t -> p (o t)"))\
                        .then_inc(sl_landed[b], 16)

            for b in range(2):
                pair_load(b, b)
            with sp.Fori(0, SBH // 4 - 1) as i:
                for b in range(2):
                    sp.wait_ge(s_o, 32 * i + 16 * (b + 1))
                    sp.wait_ge(sl_landed[b], 64 * (i + 1))
                    pair_load(b, 2 * i + 2 + b)
            for t in range(2, KD):
                panel(s_out[:, :, t * P:(t + 1) * P], KD, P)
            out_v = out.rearrange("o (t p) c -> p (o t) c", p=P)
            for k in range(KD):
                n = OUT_UNIT0 + k
                sp.wait_ge(unit_free[n % 2], n // 2 + 1)
                sp.dma_start(out_v[:, :, k * P:(k + 1) * P], f_out[:, :, k * P:(k + 1) * P]).then_inc(o_st[k % 2], 16)
            sp.wait_ge(o_st[0], 16 * KD // 2)
            sp.wait_ge(o_st[1], 16 * KD // 2)

        @block.gpsimd
        def _(g):
            ch = Tally()

            def link(ins):
                ins.then_inc(pchain, 1)
                g.wait_ge(pchain, ch.next())

            for tile, val in ((ident, 0.0), (ones, 1.0), (blk64, 0.0), (blk96, 0.0), (tri, 1.0)):
                link(nc.gpsimd.memset(tile[:, :], val))
            link(nc.gpsimd.affine_select(out=ident[:, :], in_=ident[:, :], compare_op=ALU.not_equal, fill=1.0,
                                         base=0, pattern=[[-1, P]], channel_multiplier=1))
            link(nc.gpsimd.affine_select(out=tri[:, :], in_=tri[:, :], compare_op=ALU.is_ge, fill=0.0,
                                         base=0, pattern=[[1, P]], channel_multiplier=-1))
            link(nc.gpsimd.memset(blk64[0:64, 0:64], 1 / 64))
            link(nc.gpsimd.memset(blk64[64:128, 64:128], 1 / 64))
            link(nc.gpsimd.memset(blk96[0:64, 0:64], 1 / 64))
            nc.gpsimd.memset(blk96[64:96, 64:96], 1 / 32).then_inc(consts, 1)
            g.wait_ge(consts, 1)
            link(nc.gpsimd.memset(na_mask[:, :], 0.0))
            for r0 in (0, 64):
                lo, hi = na_mask[r0:r0 + 64, 0:48], na_mask[r0:r0 + 64, 16:64]
                link(nc.gpsimd.affine_select(out=lo, in_=lo, compare_op=ALU.is_ge, fill=NEG, base=8,
                                             pattern=[[1, 48]], channel_multiplier=-1))
                link(nc.gpsimd.affine_select(out=hi, in_=hi, compare_op=ALU.is_ge, fill=NEG, base=7 - 16,
                                             pattern=[[-1, 48]], channel_multiplier=1))
            nc.gpsimd.memset(rp[:, :], 0.0).then_inc(rp_zero, 1)
            g.wait_ge(rp_zero, 1)
            g.dma_start(rp[0:60, 48:79], a["na_rpb"].rearrange("o h r c -> (o h r) c")).then_inc(rp_landed, 16)
            g.wait_ge(rp_landed, 16)
            nrow = NAH * (2 * KR - 1)
            g.dma_start(scr_bias, rp[0:nrow, :].unsqueeze(1).broadcast_to([nrow, GRID, P])).then_inc(rp_spread, 16)
            pc = Cursor()

            def ada_load(src):
                p, n = pc.at()
                if pc.n >= 2:
                    if ada_tally.n - 1 <= ADA_COLUMNS:
                        g.wait_ge(ada_col, ada_tally.n - 1)
                    else:
                        g.wait_ge(ada_acc_s, ada_tally() - 1 - ADA_COLUMNS)
                g.dma_start(ada_w[:, p, :, :], src).then_inc(ada_landed[p], 16)
                pc.n += 1
                ada_tally.n += 1

            ada_tally = Tally()
            w_ada = a["w_ada"].rearrange("o (k p) c -> p (o k) c", p=P)
            for j in range(48):
                ada_load(w_ada[:, :, j * P:(j + 1) * P])
                if j == 47:
                    g.wait_ge(rp_spread, 16)
                    g.wait_ge(unit_done[1], len(WIN_UNITS) // 2)
                    for r0, s0 in ((0, 0), (64, 1)):
                        for hh in range(NAH):
                            g.dma_start(b2[r0:r0 + 64, hh, s0:s0 + 15, :],
                                        bass.AP(scr_bias.tensor, scr_bias.offset + GRID - 1 + hh * 15 * GRID * P,
                                                [[P - 1, GRID], [GRID * P, 15], [1, GRID]])).then_inc(b2_landed, 16)
            ada2 = a["ada_w_2"].rearrange("l (k p) c -> p l k c", p=P)
            kva = a["kv_ada_w_2"].rearrange("(k p) c -> p k c", p=P)
            g.wait_ge(h_ready, 2 * KD)
            with g.Fori(0, 8) as i:
                pc.enter(i, 8)
                ada_tally.enter(i, 8)
                for l in range(2):
                    for j in range(3):
                        ada_load(ada2[:, l, :, bass.ds((3 * i + j) * P, P)])
                for j in range(2):
                    ada_load(kva[:, :, bass.ds((2 * i + j) * P, P)])
            pc.leave(8)
            ada_tally.leave(8)
            g.wait_ge(h_ready, 4 * KD)
            g.dma_start(d_row[:, :], a["m_d_2"].broadcast_to([P, NH])).then_inc(d_landed, 16)

            sx = Tally()
            with counted(g, NG, [(sx, 3 * TT - 1)]) as i:
                for c in range(TT):
                    b = c % 2
                    x3 = xt[:, c, :].rearrange("p (h d) -> p h d", h=8)
                    if c == 0:
                        g.wait_ge(ag_done, i + 1)
                        g.wait_ge(cv_tok, 9 * i + 9)
                        g.wait_ge(cv_act, 6 * i + 6)
                    for k, dst in enumerate((xdt, xw, xd)):
                        if dst is xw and c == TT - 1:
                            continue
                        if dst is xdt and c >= 2:
                            g.wait_ge(ss_y, TT * i + c - 1)
                        if dst is xw and c >= 2:
                            g.wait_ge(ss_s, (TT - 1) * i + c - 1)
                        if dst is xd and c >= 2:
                            g.wait_ge(ss_sq, TT * i + c - 1)
                        col = pool_t[:, k, 8 * c:8 * c + 8]
                        nc.gpsimd.tensor_tensor(dst[:, b, :].rearrange("p (h d) -> p h d", h=8), x3,
                                                col.unsqueeze(2).broadcast_to([P, 8, HD]), ALU.mult).then_inc(ss_x, 1)
                        g.wait_ge(ss_x, sx.next())
            g.wait_ge(o_mask, 1)
            link(nc.gpsimd.memset(tril[:, :], 1.0))
            link(nc.gpsimd.affine_select(out=tril[:, :], in_=tril[:, :], compare_op=ALU.is_ge, fill=0.0,
                                         base=-1, pattern=[[-1, P]], channel_multiplier=1))
            link(nc.gpsimd.memset(later[:, :], 0.0))
            link(nc.gpsimd.affine_select(out=later[:, T - P:T], in_=later[:, T - P:T], compare_op=ALU.is_ge, fill=1.0,
                                         base=-1, pattern=[[-1, P]], channel_multiplier=1))
            mk_ = Tally()
            with counted(g, SBH // 4, [(mk_, 32)]) as i:
                for n in range(32):
                    qt, b = n % 8, n % 2
                    g.wait_ge(s_sg, mk_(1))
                    blk = slice(qt * P, (qt + 1) * P)
                    nc.gpsimd.tensor_tensor(s_sig[:, n % 3, blk], s_sig[:, n % 3, blk], tril[:, :], ALU.mult).then_inc(s_mk, 1)
                    g.wait_ge(s_mk, mk_.next())

        @block.tensor
        def _(pe):
            pc, uc = Cursor(), Cursor()
            mm = nc.tensor.matmul

            def panel_ready():
                p, n = pc.at()
                pe.wait_ge(w_split[p], n + 1)
                return p

            def unit_open():
                p, n = uc.at()
                if uc.n >= 2:
                    pe.wait_ge(unit_free[p], n)
                return p

            def unit_close(ins):
                p, _ = uc.at()
                ins.then_inc(unit_done[p], 1)
                uc.n += 1

            def feat_unit(wp, c0, width, kt, aH, aL, panel_last=True, mid=None):
                stride = 1024 // kt if width == P else width
                up = unit_open()
                for half in range(2):
                    cols = slice(half * 512, (half + 1) * 512)
                    for k in range(kt):
                        w0 = k * stride + c0
                        whi = w_hi_t[:, wp, w0:w0 + width]
                        wlo = w_lo_t[:, wp, w0:w0 + width]
                        mm(PU[0:width, up, half, :], whi, aH[:, k, cols], start=k == 0, stop=False)
                        mm(PU[0:width, up, half, :], whi, aL[:, k, cols], start=False, stop=False)
                        last = mm(PU[0:width, up, half, :], wlo, aH[:, k, cols], start=False, stop=k == kt - 1)
                    if half == 0 and mid is not None:
                        mid()
                if panel_last:
                    pc.n += 1
                unit_close(last)

            def tok_unit(wp, aH, aL, mid=None):
                up = unit_open()
                for half in range(2):
                    for t4 in range(4):
                        t = half * 4 + t4
                        o = PU[:, up, half, t4 * P:(t4 + 1) * P]
                        tok = slice(t * P, (t + 1) * P)
                        for k in range(KD):
                            whi = w_hi_t[:, wp, k * P:(k + 1) * P]
                            wlo = w_lo_t[:, wp, k * P:(k + 1) * P]
                            mm(o, aH[:, k, tok], whi, start=k == 0, stop=False)
                            mm(o, aH[:, k, tok], wlo, start=False, stop=False)
                            last = mm(o, aL[:, k, tok], whi, start=False, stop=k == KD - 1)
                    if half == 0 and mid is not None:
                        mid()
                pc.n += 1
                unit_close(last)

            stat, sq, std = Tally(), Tally(), Tally()

            def stat_sum(src, lhsT, rows=P, r0=0, first=True, final=True):
                pe.wait_ge(sq_ready, sq.next())
                if first and stat.n:
                    pe.wait_ge(std_ready, stat())
                for half in range(2):
                    last = mm(PM[r0:r0 + rows, half, :], lhsT, src[r0:r0 + rows, half * 512:(half + 1) * 512],
                              start=first, stop=final)
                last.then_inc(stat_done, 1)
                if final:
                    stat.next()

            job = Tally()

            def ada_column(cv):
                n = job.next()
                s = (job.n - 1) % 2
                pe.wait_ge(ada_landed[s], 16 * ((job.n + 1) // 2))
                if job.n > 2:
                    pe.wait_ge(ada_mod, n - 2)
                for k in range(KD):
                    last = mm(PM[:, 2 + s, 0:1], ada_w[:, s, k, :], cv[:, k:k + 1], start=k == 0, stop=k == KD - 1)
                last.then_inc(ada_col, 1)

            def ada_job():
                n = job.next()
                pe.wait_ge(ada_acc_s, n - ADA_COLUMNS)
                if job.n > 2:
                    pe.wait_ge(ada_mod, n - 2)
                s = (job.n - 1) % 2
                mm(PM[:, 2 + s, 0:1], ada_acc[:, s, :], ones[:, 0:1], start=True, stop=True).then_inc(ada_col, 1)

            hr = Tally()

            cr = Tally()

            def spread(inv, rows=P):
                pe.wait_ge(c_inv, cr.next())
                for t in range(TT):
                    lhsT = inv[:, t:t + 1].broadcast_to([P, rows]) if inv is not inv3 else inv3[:, t, 0:rows]
                    last = mm(PM[0:rows, t // 4, (t % 4) * P:(t % 4 + 1) * P], lhsT, ident[:, :], start=True, stop=True)
                last.then_inc(c_bc, 1)

            def model_norm(between=None):
                for k in range(KD):
                    pe.wait_ge(sq_ready, sq.next())
                    if k == 0 and stat.n:
                        pe.wait_ge(std_ready, stat())
                    for t in range(TT):
                        last = mm(PM[:, 0, t:t + 1], n_sq[:, k % 2, t * P:(t + 1) * P], ones[:, 0:1],
                                  start=k == 0 and t == 0, stop=k == KD - 1 and t == TT - 1)
                    last.then_inc(stat_done, 1)
                stat.next()
                if between is not None:
                    between()
                spread(rt[:, 0, :])

            pe.wait_ge(consts, 1)
            pe.wait_ge(vec_dma, 16 * N_VEC_DMA)
            for n in range(NVEC):
                last = nc.tensor.transpose(PM[:, 2, n * P:(n + 1) * P], v_stage[:, n, :], ident[:, :])
            last.then_inc(vec_t, 1)
            for t in range(TT):
                pe.wait_ge(x_landed[t], 16)
                if t >= 2:
                    pe.wait_ge(x_ev[t % 2], t // 2)
                for k in range(KD):
                    last = nc.tensor.transpose(PU[:, t % 2, k // 4, (k % 4) * P:(k % 4 + 1) * P],
                                               x_stage[:, t, k * P:(k + 1) * P], ident[:, :])
                last.then_inc(x_t, 1)
            pe.wait_ge(cact_done, 1)
            model_norm(lambda: [ada_column(cact[:, 0:8]) for _ in range(16)])
            pe.wait_ge(h_ready, hr.next(KD))
            later = []
            for n, (kind, t, c0) in enumerate(WIN_UNITS):
                wp = panel_ready()
                mids = list(later)
                later = []

                def mid(todo=mids):
                    for f in todo:
                        f()

                if n == 0:
                    pe.wait_ge(x_ev[0], TT // 2)
                    pe.wait_ge(x_ev[1], TT // 2)
                if kind == "v":
                    tok_unit(wp, hH, hL, mid)
                elif kind == "krope":
                    feat_unit(wp, 0, ROPE, KD, hH, hL, mid=mid)
                else:
                    feat_unit(wp, 0, P, KD, hH, hL, mid=mid)
                if kind in ("q", "k"):
                    later.append(lambda: stat_sum(j_sq[:, :], blk64[:, :]))
                if kind == "cq":
                    later.append(lambda t=t: stat_sum(j_sq[:, :], ones[:, :], first=t == 0, final=t == 2))
                if kind == "ckv":
                    later.append(lambda t=t: stat_sum(j_sq[:, :], ones[:, :], first=t == 0, final=t == 1))
                for _ in range(ADA_AT_UNIT[n]):
                    ada_job()
            stat_sum(j_sq[:, :], blk96[64:96, 64:96], rows=ROPE, r0=64)

            def na_scores(n, j, i):
                hp, pair = j // 8, j % 8
                s0, _ = NA_PAIRS[pair]
                wide = 2 <= pair <= 5
                if pair == 0:
                    pe.wait_ge(na_stage, (2 * i + hp) + 1)
                    pe.wait_ge(na_kstage, (2 * i + hp) + 1)
                b = j % 2
                q = na_qs[:, hp, pair * P:(pair + 1) * P]
                last = mm(PU[:, b, 0, :], q, na_ks[:, hp, s0 * GRID:s0 * GRID + 512], start=True, stop=True)
                if wide:
                    last = mm(PU[:, b, 1, 0:64], q, na_ks[:, hp, s0 * GRID + 512:s0 * GRID + 576], start=True, stop=True)
                last.then_inc(na_s, 1)

            def na_transposes(j):
                pair = j % 8
                wide = 2 <= pair <= 5
                for c in range(4):
                    last = nc.tensor.transpose(PM[:, 0, c * P:(c + 1) * P], na_p[:, j % 2, c * P:(c + 1) * P], ident[:, :])
                if wide:
                    last = nc.tensor.transpose(PM[0:64, 1, 0:P], na_p[:, j % 2, 512:576], ident[:, :])
                last.then_inc(na_tr, 1)

            def na_values(i, j):
                hp, pair = j // 8, j % 8
                s0, _ = NA_PAIRS[pair]
                wide = 2 <= pair <= 5
                o = PM[:, 2 + j % 2, 0:HD]
                vc = bass.ds((2 * i + hp) * HD, HD)
                for c in range(4):
                    last = mm(o, na_pt[:, j % 2, c, :], na_v[:, s0 // 2 + c, vc], start=c == 0, stop=c == 3 and not wide)
                if wide:
                    last = mm(o, na_pt[0:64, j % 2, 4, :], na_v[0:64, s0 // 2 + 4, vc], start=False, stop=True)
                last.then_inc(na_pv, 1)

            NS = 16
            with pe.Fori(0, NAH // 2) as i:
                for j in range(NS + 2):
                    if j < NS:
                        if j >= 2:
                            pe.wait_ge(na_l, i * NS + j - 1)
                        na_scores(None, j, i)
                    if j >= 2:
                        pe.wait_ge(na_ev, i * NS + j - 1)
                        if j >= 4:
                            pe.wait_ge(na_o, i * NS + j - 3)
                        na_values(i, j - 2)
                    if 1 <= j <= NS:
                        pe.wait_ge(na_e, i * NS + j)
                        if j >= 2:
                            pe.wait_ge(na_ev, i * NS + j - 1)
                        na_transposes(j - 1)

            pe.wait_ge(wu_landed, 32)
            pe.wait_ge(na_o, 2 * NS)
            pe.wait_ge(j_done, 3)

            def head_rows(wt, kt, src, c0, rows):
                up = unit_open()
                for half in range(2):
                    for k in range(kt):
                        last = mm(PU[0:rows, up, half, :], wt[:, k, c0:c0 + rows], src[:, k, half * 512:(half + 1) * 512],
                                  start=k == 0, stop=k == kt - 1)
                unit_close(last)

            pe.wait_ge(std_ready, stat())
            for n in range(2 * MH + 2):
                if n < MH:
                    head_rows(wuq, 3, cq, n * 96, 96)
                elif n < 2 * MH:
                    head_rows(wukv, 2, ckv, (n - MH) * P, HD)
                if 1 <= n <= 2 * MH:
                    rows = 96 if n <= MH else HD
                    pe.wait_ge(sq_ready, sq.next())
                    for t in range(TT):
                        last = mm(PM[:, 2 + n % 2, 3 * t:3 * t + 3], u_sq[0:rows, t * P:(t + 1) * P], blk96[0:rows, 0:96:32],
                                  start=True, stop=True)
                    last.then_inc(c_sum, 1)
                if n >= 2:
                    if n >= 3:
                        pe.wait_ge(h_app, n - 2)
                    spread(inv3, 96 if n - 2 < MH else HD)
            wv = wukv[:, :, :].rearrange("p k (h c) -> p k h c", h=MH)
            for n in range(TT // 2):
                up = unit_open()
                for t2 in range(2):
                    t = 2 * n + t2
                    for k in range(2):
                        last = mm(PU[:, up, t2, :], ckv[:, k, t * P:(t + 1) * P], wv[:, k, :, HD:2 * HD],
                                  start=k == 0, stop=k == 1)
                unit_close(last)
            pe.wait_ge(unit_free[(uc.n - 1) % 2], (uc.n + 1) // 2)
            pe.wait_ge(unit_free[uc.n % 2], uc.n // 2)
            pe.wait_ge(j_done, 3 + MH)
            pe.wait_ge(mh_done, MH)
            pe.wait_ge(h_app, 2 * MH)
            with pe.Fori(0, MH) as i:
                for j in range(TT + 2):
                    b = j % 2
                    if j < TT:
                        pe.wait_ge(mla_q, i * TT + j + 1)
                        if j >= 2:
                            pe.wait_ge(mla_e, i * TT + j - 1)
                        for half in range(2):
                            last = mm(PU[:, b, half, :], m_qs[0:96, b, :],
                                      mk[0:96, bass.ds(i, 1), half * 512:(half + 1) * 512], start=True, stop=True)
                        last.then_inc(mla_s, 1)
                    if j >= 2:
                        pe.wait_ge(mla_ev, i * TT + j - 1)
                        if j >= 4:
                            pe.wait_ge(mla_o, i * TT + j - 3)
                        o = PM[:, 2 + b, 0:HD]
                        for c in range(TT):
                            last = mm(o, m_pt[:, b, c, :], mv[:, c, bass.ds(i * HD, HD)], start=c == 0, stop=c == TT - 1)
                        last.then_inc(mla_pv, 1)
                    if 1 <= j <= TT:
                        b1 = (j - 1) % 2
                        pe.wait_ge(mla_e, i * TT + j)
                        if j >= 2:
                            pe.wait_ge(mla_ev, i * TT + j - 1)
                        for c in range(TT):
                            last = nc.tensor.transpose(PM[:, c // 4, (c % 4) * P:(c % 4 + 1) * P],
                                                       m_p[:, b1, c * P:(c + 1) * P], ident[:, :])
                        last.then_inc(mla_tr, 1)

            for t in range(2):
                stat_sum(g_t[:, t, :], blk64[:, :])
            for f in range(6):
                pe.wait_ge(y_norm, 1 if f < 2 else 2)
                up = unit_open()
                src = y_na if f < 2 else y_mla
                fc = (f if f < 2 else f - 2) * P
                for t in range(TT):
                    last = nc.tensor.transpose(PU[:, up, t // 4, (t % 4) * P:(t % 4 + 1) * P],
                                               src[:, t, fc:fc + P], ident[:, :])
                unit_close(last)
            pe.wait_ge(h_ready, hr.next(KD))
            for t in range(KD):
                feat_unit(panel_ready(), 0, P, KD, hH, hL)
            model_norm()
            pe.wait_ge(h_ready, hr.next(KD))
            fa = Tally()

            def down():
                pe.wait_ge(f_act, fa.next(2))
                for c in range(2):
                    wp = panel_ready()
                    for u in range(4):
                        feat_unit(wp, u * P, P, 2, f_hi, f_lo, panel_last=u == 3)

            def gate_up():
                feat_unit(panel_ready(), 0, P, KD, hH, hL)

            def ffn_body(i, times, jobs):
                pc.enter(i, 6)
                uc.enter(i, 12)
                fa.enter(i, 2)
                job.enter(i, jobs)
                for n in range(4):
                    if n == 3:
                        down()
                    gate_up()
                    for _ in range(jobs // 4):
                        ada_job()
                pc.leave(times)
                uc.leave(times)
                fa.leave(times)
                job.leave(times)

            for _ in range(4):
                gate_up()
            with pe.Fori(0, 8) as i:
                ffn_body(i, 8, 8)
            with pe.Fori(0, FT // 2 - 9) as i:
                ffn_body(i, FT // 2 - 9, 0)
            down()

            model_norm()
            pe.wait_ge(h_ready, hr.next(KD))
            feat_unit(panel_ready(), 0, NH, KD, hH, hL)
            pe.wait_ge(dt_f, 1)
            for w in range(2):
                for t in range(TT):
                    last = nc.tensor.transpose(PM[:, w, t * NH:(t + 1) * NH], dt_w[:, 2 + w, t * P:(t + 1) * P],
                                               ident[0:NH, 0:NH])
            last.then_inc(dt_t_s, 1)
            pe.wait_ge(dt_tok, 1)
            mm(PM[:, 2, 0:256], tri[:, :], a_t[:, :, :], start=True, stop=True)
            mm(PM[:, 2, 256:512], ones[:, :], a_t[:, :, :], start=True, stop=True).then_inc(dt_sum, 1)
            pe.wait_ge(dt_log, 1)
            with counted(pe, NG, [(pc, 14), (uc, 22)]) as i:
                for j in range(11):
                    if j < 10:
                        feat_unit(panel_ready(), 0, P, KD, hH, hL)
                    if j and j != 6:
                        if j < 6:
                            pe.wait_ge(cv_act, 6 * i + j)
                        else:
                            zp, zn = uc.at(-2 if j < 10 else -1)
                            pe.wait_ge(unit_free[zp], zn + 1)
                        n = j - 1 if j < 6 else j - 2
                        if n:
                            pe.wait_ge(cv_tok, 9 * i + n)
                        src = bT if j == 5 else c_out[:, (j - 1) % 2, :]
                        for t in range(TT):
                            last = nc.tensor.transpose(PM[:, t // 4, (t % 4) * P:(t % 4 + 1) * P],
                                                       src[:, t * P:(t + 1) * P], ident[:, :])
                        last.then_inc(cv_tr, 1)
                pe.wait_ge(ag_done, i + 1)
                pe.wait_ge(cv_act, 6 * i + 6)
                pe.wait_ge(cv_tok, 9 * i + 9)
                for j in range(TT + 1):
                    if j < TT:
                        tok = slice(j * P, (j + 1) * P)
                        if j:
                            pe.wait_ge(ss_cbr, TT * i + j)
                        mm(PU[:, 1, 1, 0:P], bT[:, tok], cT[:, tok], start=True, stop=True)
                        for h in range(8):
                            last = mm(PU[:, 0, h // 4, (h % 4) * P:(h % 4 + 1) * P],
                                      ag[:, j, h:h + 1].broadcast_to([P, P]), tri[:, :], start=True, stop=True)
                        last.then_inc(ss_bc, 1)
                    if j < TT - 1:
                        pe.wait_ge(ss_x, (3 * TT - 1) * i + 3 * j + 2)
                        if j:
                            pe.wait_ge(ss_st, (TT - 1) * i + j)
                        mm(PU[:, 1, 0, :], bt[:, j, :], xw[:, j % 2, :], start=True, stop=True).then_inc(ss_s, 1)
                    if j:
                        c = j - 1
                        b = c % 2
                        if c >= 2:
                            pe.wait_ge(ss_g, TT * i + c - 1)
                        if c:
                            pe.wait_ge(ss_st, (TT - 1) * i + c)
                            mm(PM[:, 2 + b, :], cT[:, c * P:(c + 1) * P], state[:, 1 - b, :], start=True, stop=True)\
                                .then_inc(ss_off, 1)
                        pe.wait_ge(ss_m, TT * i + c + 1)
                        pe.wait_ge(ss_x, (3 * TT - 1) * i + 3 * c + 1)
                        for h in range(8):
                            last = mm(PM[:, b, h * HD:(h + 1) * HD], seg[:, b, h, :], xdt[:, b, h * HD:(h + 1) * HD],
                                      start=True, stop=True)
                        last.then_inc(ss_y, 1)
                pe.wait_ge(m_norm, i + 1)
                for f in range(4):
                    up = unit_open()
                    for t in range(TT):
                        last = nc.tensor.transpose(PU[:, up, t // 4, (t % 4) * P:(t % 4 + 1) * P],
                                                   zt[:, t, f * P:(f + 1) * P], ident[:, :])
                    unit_close(last)
                pe.wait_ge(y_lo_s, 4 * i + 4)
                for c in range(4):
                    wp = panel_ready()
                    for u in range(2):
                        feat_unit(wp, u * P, P, 4, y_hi, y_lo, panel_last=u == 1)
            model_norm()
            for w in range(2):
                pe.wait_ge(h_ready, hr.next(KD))
                with counted(pe, KD, [(pc, 2), (uc, 2)]) as i:
                    feat_unit(panel_ready(), 0, P, KD, hH, hL)
                    feat_unit(panel_ready(), 0, P, KD, hH, hL)
                    if w == 0:
                        vp, vn = uc.at(-2)
                        pe.wait_ge(unit_free[vp], vn + 1)
                        pe.wait_ge(v_ev, i + 1)
                        for t in range(TT):
                            last = nc.tensor.transpose(PM[:, t // 4, (t % 4) * P:(t % 4 + 1) * P],
                                                       v_f[:, t * P:(t + 1) * P], ident[:, :])
                        last.then_inc(v_tr, 1)

            for back in (1, 2):
                zp, zn = uc.at(-back)
                pe.wait_ge(unit_free[zp], zn + 1)
            NS = 32
            with pe.Fori(0, SBH // 4) as i:
                for j in range(NS + 3):
                    if j < NS:
                        pb, hd, qt, b = j // 16, (j // 8) % 2, j % 8, j % 2
                        r = slice(hd * HD, (hd + 1) * HD)
                        if j % 16 == 0:
                            pe.wait_ge(sl_landed[pb], 64 * (i + 1))
                        if j >= 2:
                            pe.wait_ge(s_sg, NS * i + j - 1)
                        for half in range(1 + qt // 4):
                            w = min((qt + 1) * P, (half + 1) * 512)
                            last = mm(PU[:, b, half, 0:w - half * 512], s_q[r, pb, qt * P:(qt + 1) * P],
                                      s_k[r, pb, half * 512:w], start=True, stop=True)
                        last.then_inc(s_s, 1)
                    if j >= 3:
                        n = j - 3
                        pb, hd, qt = n // 16, (n // 8) % 2, n % 8
                        pe.wait_ge(s_ev[n % 2], NS // 2 * i + n // 2 + 1)
                        if n >= 2:
                            pe.wait_ge(s_o, NS * i + n - 1)
                        for c in range(qt + 1):
                            last = mm(PM[hd * HD:(hd + 1) * HD, 2 + n % 2, 0:P], s_v[:, pb, c, hd * HD:(hd + 1) * HD],
                                      s_at[:, n % 2, c, :], start=c == 0, stop=c == qt)
                        last.then_inc(s_pv, 1)
                    if 2 <= j <= NS + 1:
                        n = j - 2
                        pe.wait_ge(s_a, NS * i + n + 1)
                        if n:
                            pe.wait_ge(s_ev[(n - 1) % 2], NS // 2 * i + (n - 1) // 2 + 1)
                        for c in range(n % 8 + 1):
                            last = nc.tensor.transpose(PM[:, c // 4, (c % 4) * P:(c % 4 + 1) * P],
                                                       s_sig[:, n % 3, c * P:(c + 1) * P], ident[:, :])
                        last.then_inc(s_tr, 1)
            pe.wait_ge(ep_lo, KD)
            for t in range(KD):
                feat_unit(panel_ready(), 0, P, KD, hH, hL)
            model_norm()
            for k in range(KD):
                pe.wait_ge(o_xn, k + 1)
                up = unit_open()
                for t in range(TT):
                    last = nc.tensor.transpose(PU[:, up, t // 4, (t % 4) * P:(t % 4 + 1) * P],
                                               n_x[:, k % 2, t * P:(t + 1) * P], ident[:, :])
                unit_close(last)

        @block.scalar
        def _(act):
            pc, uc = Cursor(), Cursor()
            ch = Tally()
            af = nc.scalar.activation

            def link(ins):
                ins.then_inc(achain, 1)
                act.wait_ge(achain, ch.next())

            def split():
                p, n = pc.at()
                act.wait_ge(w_landed[p], 16 * (n + 1))
                if pc.n >= 2:
                    lp, ln = uc.at(-1)
                    act.wait_ge(unit_done[lp], ln + 1)
                w = SPLIT_W(pc)
                af(w_hi_t[:, p, 0:w], w_raw[:, p, 0:w], ACT.Copy).then_inc(w_hi[p], 1)
                pc.n += 1

            def SPLIT_W(c):
                return KD * ROPE if c.i is None and c.n in NARROW else 1024

            def unit():
                p, n = uc.at()
                act.wait_ge(unit_done[p], n + 1)
                return p

            def free(ins):
                p, _ = uc.at()
                ins.then_inc(unit_free[p], 1)
                uc.n += 1

            def skip():
                uc.n += 1

            stat, sqt, std, cr = Tally(), Tally(), Tally(), Tally()

            def root(dst, scale=1.0, rows=P, r0=0, sums=1):
                act.wait_ge(stat_done, stat.next(sums))
                af(dst[r0:r0 + rows, :], stat_ps[r0:r0 + rows, :], ACT.Sqrt, bias=EPS, scale=scale).then_inc(std_ready, 1)
                std.next()

            def model_norm(residual=0):
                for k in range(KD):
                    if residual:
                        rp_, rn = uc.at(k - residual)
                        act.wait_ge(unit_free[rp_], rn + 1)
                    if k >= 2:
                        act.wait_ge(stat_done, stat(k - 1))
                    af(n_sq[:, k % 2, :], xT[:, k, :], ACT.Square).then_inc(sq_ready, 1)
                act.wait_ge(stat_done, stat.next(KD))
                af(rt[:, 0, 0:TT], PM[:, 0, 0:TT], ACT.Sqrt, bias=EPS, scale=1 / D).then_inc(c_root, 1)
                act.wait_ge(c_bc, cr.next())
                af(n_rs[:, :], stat_ps, ACT.Copy).then_inc(std_ready, 1)
                std.next()

            ht = Tally()

            def h_high():
                for k in range(KD):
                    act.wait_ge(h_tmp, ht.next())
                    af(hH[:, k, :], n_h[:, k % 2, :], ACT.Copy).then_inc(h_hi, 1)

            act.wait_ge(vec_zero, 1)
            n_dma = 0
            for name, src, rows, width in VEC_ROWS(a):
                c = VEC[name][0]
                act.dma_start(v_stage[c % P:c % P + rows, c // P, 0:width], src).then_inc(vec_dma, 16)
                n_dma += 1
            for name, src, off, width in VEC_PARTS(a):
                c = VEC[name][0]
                act.dma_start(v_stage[c % P:c % P + 1, c // P, off:off + width], src).then_inc(vec_dma, 16)
                n_dma += 1
            act.dma_start(kv_row[64:96, 0:1], a["rope_inv"]).then_inc(rope_f, 16)
            assert n_dma == N_VEC_DMA, n_dma
            act.wait_ge(vec_t, 1)
            act.wait_ge(vec_done, 1)
            af(cact[:, :], v("c", 0, 16), ACT.Silu).then_inc(cact_done, 1)
            for t in range(0, TT, 2):
                act.wait_ge(x_t, t + 1)
                af(xT[:, :, t * P:(t + 1) * P], PU[:, 0, :, :].rearrange("p a (b q) -> p (a b) q", q=P), ACT.Copy)\
                    .then_inc(x_ev[0], 1)
            act.wait_ge(x_ev[0], TT // 2)
            act.wait_ge(x_ev[1], TT // 2)
            model_norm()
            split()
            h_high()

            readers = []

            def root_job(reader, *args, **kw):
                if readers:
                    act.wait_ge(*readers[-1])
                root(*args, **kw)
                readers.append(reader)

            for n, (kind, t, c0) in enumerate(WIN_UNITS):
                split()
                if kind == "x":
                    p = unit()
                    if t == 0:
                        act.wait_ge(h_ready, KD)
                    else:
                        act.wait_ge(unit_free[1], 1)
                    free(af(conv_x[:, :], unit_ps(p), ACT.Copy))
                elif kind in ("gc", "gb"):
                    skip()
                elif kind in ("q", "k"):
                    p = unit()
                    af(j_sq[:, :], unit_ps(p), ACT.Square).then_inc(sq_ready, 1)
                    root_job((unit_free[p], uc.n // 2 + 1), j_rs)
                    skip()
                elif kind == "v":
                    p = unit()
                    free(af(na_v[:, :, t * P:(t + 1) * P], unit_ps(p).rearrange("p (t c) -> p t c", c=P), ACT.Copy))
                elif kind in ("cq", "ckv"):
                    p = unit()
                    dst, tiles = (cq, QR // P) if kind == "cq" else (ckv, KVR // P)
                    if t:
                        act.wait_ge(stat_done, stat(t))
                    af(j_sq[:, :], unit_ps(p), ACT.Square).then_inc(sq_ready, 1)
                    free(af(dst[:, t, :], unit_ps(p), ACT.Copy))
                    if t == tiles - 1:
                        root_job((j_done, 1 if kind == "cq" else 2), j_rs, 1 / (tiles * P), sums=tiles)
                else:
                    p = unit()
                    free(af(k_raw[64:96, :], unit_ps(p, ROPE), ACT.Copy))
                    act.wait_ge(unit_free[p], uc.n // 2)
                    af(j_sq[64:96, :], k_raw[64:96, :], ACT.Square).then_inc(sq_ready, 1)
                    root_job((j_done, 3), j_rs, rows=ROPE, r0=64)

            NS = 16
            with act.Fori(0, NAH // 2) as i:
                for j in range(NS + 1):
                    pair = j % 8
                    if j < NS and pair == 0:
                        hp = j // 8
                        af(na_ks[:, hp, :], na_k[hp * 64:hp * 64 + 64, bass.ds(i, 1), :].rearrange("p a b -> p (a b)"), ACT.Copy)\
                            .then_inc(na_kstage, 1)
                    if j < NS:
                        w = 576 if 2 <= pair <= 5 else 512
                        act.wait_ge(na_l, i * NS + j + 1)
                        af(na_p[:, j % 2, 0:w], na_p[:, j % 2, 0:w], ACT.Exp, bias=small[:, 8 + j % 2:9 + j % 2],
                           accum_out=small[:, 28 + j % 4:29 + j % 4]).then_inc(na_e, 1)
                    if j >= 1:
                        wide = 2 <= (j - 1) % 8 <= 5
                        act.wait_ge(na_tr, i * NS + j)
                        if j >= 3:
                            act.wait_ge(na_pv, i * NS + j - 2)
                        b1 = (j - 1) % 2
                        ins = af(na_pt[:, b1, 0:4, :], PM[:, 0, :].rearrange("p (a b) -> p a b", a=4), ACT.Copy)
                        if wide:
                            ins = af(na_pt[0:64, b1, 4, :], PM[0:64, 1, 0:P], ACT.Copy)
                        ins.then_inc(na_ev, 1)

            act.wait_ge(na_o, 2 * NS)
            act.dma_start(rope_t[64:96, :].bitcast(I32), a["positions"].broadcast_to([32, T])).then_inc(rope_dma, 16)
            act.dma_start(wuq[:, :, :], a["mla_w_uq"].rearrange("o (k p) c -> p (o k) c", p=P)).then_inc(wu_landed, 16)
            act.dma_start(wukv[:, :, :], a["mla_w_ukv"].rearrange("o (k p) c -> p (o k) c", p=P)).then_inc(wu_landed, 16)
            for w in range(2):
                act.wait_ge(rope_arg, w + 1)
                af(rope[64:96, w, :], rope[64:96, w, :], ACT.Sin).then_inc(rope_done, 1)
            for n in range(2 * MH + 1):
                if n < 2 * MH:
                    rows = 96 if n < MH else HD
                    p = unit()
                    if n:
                        act.wait_ge(c_sum, n)
                    af(u_sq[0:rows, :], unit_ps(p, rows), ACT.Square).then_inc(sq_ready, 1)
                    dst = mq if n < MH else mk
                    free(af(dst[0:rows, n % MH, :], unit_ps(p, rows), ACT.Copy))
                if n:
                    cr.next()
                    act.wait_ge(c_sum, n)
                    af(rt[:, n % 2, 0:3 * TT], PM[:, 2 + n % 2, 0:3 * TT], ACT.Sqrt, bias=EPS).then_inc(c_root, 1)
                if MH <= n < 2 * MH:
                    if n == MH:
                        act.wait_ge(rope_x, 1)
                    af(mk[64:96, n - MH, :], rope_k[64:96, :], ACT.Copy).then_inc(mh_done, 1)
            for n in range(TT // 2):
                if n == 0:
                    act.wait_ge(j_done, 3 + MH)
                p = unit()
                free(af(mv[:, 2 * n:2 * n + 2, :], PU[:, p, :, :], ACT.Copy))

            scale = float(np.float32((HD + ROPE) ** -0.5))
            with act.Fori(0, MH) as i:
                for j in range(TT + 1):
                    b = j % 2
                    if j < TT:
                        act.wait_ge(mla_m, i * TT + j + 1)
                        af(m_p[:, b, :], unit_ps(b), ACT.Exp, bias=small[:, 16 + b:17 + b], scale=scale,
                           accum_out=small[:, 32 + j % 4:33 + j % 4]).then_inc(mla_e, 1)
                    if j >= 1:
                        b1 = (j - 1) % 2
                        act.wait_ge(mla_tr, i * TT + j)
                        if j >= 3:
                            act.wait_ge(mla_pv, i * TT + j - 2)
                        af(m_pt[:, b1, :, :].rearrange("p a b -> p (a b)"), stat_ps, ACT.Copy).then_inc(mla_ev, 1)

            act.wait_ge(mla_o, MH * TT)
            for t in range(2):
                af(g_t[:, t, :], y_conv[:, t, :], ACT.Square).then_inc(sq_ready, 1)
            for t in range(2):
                root_job((h_tmp, ht(1)), u_rs)
                act.wait_ge(h_tmp, ht.next())
                af(hH[:, 6 + t, :], g_h[:, t, :], ACT.Copy).then_inc(h_hi, 1)
            af(g_sq[:, 0:2048], y_na[:, :, :].rearrange("p a b -> p (a b)"), ACT.Square).then_inc(y_sq, 1)
            act.wait_ge(y_sum, 1)
            af(g_rs[:, 0:32], g_rs[:, 0:32], ACT.Sqrt, bias=EPS, scale=1 / HD).then_inc(y_root, 1)
            af(g_sq[:, :], y_mla[:, :, :].rearrange("p a b -> p (a b)"), ACT.Square).then_inc(y_sq, 1)
            act.wait_ge(y_sum, 2)
            af(g_rs[:, 32:96], g_rs[:, 32:96], ACT.Sqrt, bias=EPS, scale=1 / HD).then_inc(y_root, 1)
            for f in range(6):
                gp, gn = uc.at()
                act.wait_ge(unit_free[gp], gn + 1)
                skip()
                af(hH[:, f, :], g_h[:, f % 2, :], ACT.Copy).then_inc(h_hi, 1)
            for t in range(KD):
                split()
                skip()
            model_norm(residual=KD)
            h_high()
            up = Tally()

            def gate(t):
                split()
                p = unit()
                free(af(f_silu[:, t, :], unit_ps(p), ACT.Silu))

            def high(t, upu):
                act.wait_ge(unit_free[upu[0]], upu[1] + 1)
                up.next()
                af(f_hi[:, t, :], f_prod[:, t, :], ACT.Copy).then_inc(f_hi_s, 1)

            def passed(units):
                split()
                for _ in range(units):
                    skip()

            def ffn_body(i, times):
                pc.enter(i, 6)
                uc.enter(i, 12)
                up.enter(i, 2)
                gate(0)
                up0 = uc.at()
                passed(1)
                gate(1)
                passed(4)
                passed(4)
                lp, ln = uc.at(-1)
                act.wait_ge(unit_done[lp], ln + 1)
                high(0, up0)
                up1 = uc.at()
                passed(1)
                high(1, up1)
                pc.leave(times)
                uc.leave(times)
                up.leave(times)

            for t in range(2):
                gate(t)
                upu = uc.at()
                passed(1)
                high(t, upu)
            with act.Fori(0, 8) as i:
                ffn_body(i, 8)
            with act.Fori(0, FT // 2 - 9) as i:
                ffn_body(i, FT // 2 - 9)
            passed(4)
            passed(4)

            model_norm(residual=KD)
            h_high()
            split()
            skip()
            act.wait_ge(dt_x, 1)
            af(dt_w[:, 1, :], dt_w[:, 1, :], ACT.Exp)
            af(small[0:NH, 40:41], v("a_log", rows=NH), ACT.Exp).then_inc(dt_x, 1)
            act.wait_ge(dt_log, 1)
            af(eacum[:, :, :], acum[:, :, :], ACT.Exp)
            af(etot[:, :, :], etot[:, :, :], ACT.Exp)
            af(wend[:, :, :], wend[:, :, :], ACT.Exp).then_inc(dt_exp, 1)
            with counted(act, NG, [(pc, 14), (uc, 22), (ch, TT)]) as i:
                def activate(j):
                    act.wait_ge(cv_done, 6 * i + j + 1)
                    dst = c_out[:, j % 2, :] if j < 4 else (bT if j == 4 else cT)[:, :]
                    af(dst, c_out[:, j % 2, :], ACT.Silu).then_inc(cv_act, 1)

                for j in range(6):
                    split()
                    if j:
                        activate(j - 1)
                    p = unit()
                    if j >= 2:
                        act.wait_ge(cv_done, 6 * i + j - 1)
                    free(af(c_raw[:, j % 2, 3:3 + T], unit_ps(p), ACT.Copy))
                    if j:
                        act.wait_ge(cv_tr, 9 * i + j)
                        dst = bt[:, :, :] if j == 5 else xt[:, :, (j - 1) * P:j * P]
                        af(dst, stat_ps.rearrange("p (t c) -> p t c", c=P), ACT.Copy).then_inc(cv_tok, 1)
                for j in range(5):
                    if j < 4:
                        split()
                        if j == 0:
                            activate(5)
                        p = unit()
                        if j < 2:
                            act.wait_ge(cv_act, 6 * i + 5 + j)
                        else:
                            act.wait_ge(cv_tr, 9 * i + 4 + j)
                        free(af(c_out[:, j % 2, :], unit_ps(p), ACT.Silu))
                    if j:
                        act.wait_ge(cv_tr, 9 * i + 5 + j)
                        af(zt[:, :, (j - 1) * P:j * P], stat_ps.rearrange("p (t c) -> p t c", c=P), ACT.Copy).then_inc(cv_tok, 1)
                for j in range(TT + 1):
                    if j < TT:
                        act.wait_ge(ss_seg, TT * i + j + 1)
                        s2 = seg[:, j % 2, :, :].rearrange("p h t -> p (h t)")
                        link(af(s2, s2, ACT.Relu, scale=-1.0))
                        af(s2, s2, ACT.Exp, scale=-1.0).then_inc(ss_exp, 1)
                    if j:
                        act.wait_ge(ss_g, TT * i + j)
                        af(xd[:, (j - 1) % 2, :], zt[:, j - 1, :], ACT.Square, accum_out=m_ss[:, j - 1:j]).then_inc(ss_sq, 1)
                act.wait_ge(ss_sq, TT * i + TT)
                af(m_ss[:, :], m_ss[:, :], ACT.Sqrt, bias=EPS, scale=1 / 512).then_inc(m_root, 1)
                for f in range(4):
                    gp, gn = uc.at()
                    act.wait_ge(unit_free[gp], gn + 1)
                    skip()
                    af(y_hi[:, f, :], y_t32[:, f % 2, :], ACT.Copy).then_inc(y_hi_s, 1)
                for c in range(4):
                    passed(2)
            model_norm(residual=KD)
            for w in range(2):
                h_high()
                def store(k, i):
                    act.dma_start(scr_heads[k][bass.ds(i, 1), :, :].rearrange("o p t -> p (o t)"), stage[:, k, :])\
                        .then_inc(st_done[k], 16)

                with counted(act, KD, [(pc, 2), (uc, 2)]) as i:
                    if w == 0:
                        split()
                        p = unit()
                        free(af(v_f[:, :], unit_ps(p), ACT.Copy))
                        split()
                        skip()
                        kp, kn = uc.at(-1)
                        act.wait_ge(unit_free[kp], kn + 1)
                        store(0, i)
                        act.wait_ge(v_ev, i + 2)
                        store(1, i)
                    else:
                        split()
                        skip()
                        split()
                        p = unit()
                        qp, qn = uc.at(-1)
                        free(af(stage[:, 3, :], unit_ps(p), ACT.Silu))
                        act.wait_ge(unit_free[qp], qn + 1)
                        store(2, i)
                        zp, zn = uc.at(-1)
                        act.wait_ge(unit_free[zp], zn + 1)
                        store(3, i)
                        act.wait_ge(st_done[3], 16 * (i + 1))
            NS = 32
            with act.Fori(0, SBH // 4) as i:
                for j in range(NS + 3):
                    if j < NS:
                        qt, b = j % 8, j % 2
                        w = (qt + 1) * P
                        act.wait_ge(s_s, NS * i + j + 1)
                        if j >= 2:
                            act.wait_ge(s_a, NS * i + j - 1)
                        if j >= 3:
                            act.wait_ge(s_tr, NS * i + j - 2)
                        af(s_sig[:, j % 3, 0:w], unit_ps(b)[:, 0:w], ACT.Sigmoid, scale=HD ** -0.5)
                        af(s_keep[:, b, 0:w], unit_ps(b)[:, 0:w], ACT.Sigmoid, scale=-HD ** -0.5).then_inc(s_sg, 1)
                    n = j - 2
                    if 0 <= n < NS and n % 2:
                        act.wait_ge(s_tr, NS * i + n + 1)
                        if n >= 2:
                            act.wait_ge(s_pv, NS * i + n - 1)
                        w = (n % 8 + 1) * P
                        af(s_at[:, 1, :, :].rearrange("p a b -> p (a b)")[:, 0:w], stat_ps[:, 0:w], ACT.Copy)\
                            .then_inc(s_ev[1], 1)
                    if j in (19, NS + 2):
                        pb = j // 32
                        act.wait_ge(s_o, NS * i + 16 * (pb + 1))
                        af(hH[:, bass.ds(2 * i + pb, 1), :].rearrange("p a b -> p (a b)"), s_of[:, pb, :], ACT.Copy)\
                            .then_inc(ep_hi, 1)
            for t in range(KD):
                if t < KD - 1:
                    split()
                skip()
            model_norm(residual=KD)
            for k in range(KD):
                p = unit()
                free(af(f_out[:, :, k * P:(k + 1) * P], unit_ps(p).rearrange("p (t c) -> p t c", c=P), ACT.Copy))

        @block.vector
        def _(ve):
            pc, uc = Cursor(), Cursor()
            ch = Tally()
            V = nc.vector

            def link(ins):
                ins.then_inc(vchain, 1)
                ve.wait_ge(vchain, ch.next())

            def split():
                p, n = pc.at()
                ve.wait_ge(w_hi[p], n + 1)
                w = KD * ROPE if pc.i is None and pc.n in NARROW else 1024
                V.tensor_tensor(w_lo_t[:, p, 0:w], w_raw[:, p, 0:w], w_hi_t[:, p, 0:w].bitcast(F32), ALU.subtract)\
                    .then_inc(w_split[p], 1)
                pc.n += 1

            def unit():
                p, n = uc.at()
                ve.wait_ge(unit_done[p], n + 1)
                return p

            def free(ins):
                p, _ = uc.at()
                ins.then_inc(unit_free[p], 1)
                uc.n += 1

            def skip(n=1):
                uc.n += n

            job = Tally()

            pending = []

            def ada_finish():
                n, s, col, bias = pending.pop(0)
                ve.wait_ge(ada_col, n)
                V.tensor_tensor(mod[:, bass.ds(col, 1)], PM[:, 2 + s, 0:1], vec[:, bass.ds(bias, 1)], ALU.add).then_inc(ada_mod, 1)

            def ada_job(cv, col, bias):
                n = job.next()
                s = (job.n - 1) % 2
                jm = (job.n - 1) // 2 + (0 if job.i is None else job.i * (job.per // 2))
                ve.wait_ge(ada_landed[s], 16 * (jm + 1))
                if job.n > 2:
                    ve.wait_ge(ada_col, n - 2)
                link(V.tensor_scalar(ada_acc[:, s, :], ada_w[:, s, 0, :], cv[:, 0:1], None, ALU.mult))
                for k in range(1, KD):
                    ins = V.scalar_tensor_tensor(ada_acc[:, s, :], ada_w[:, s, k, :], cv[:, k:k + 1], ada_acc[:, s, :],
                                                 ALU.mult, ALU.add)
                    if k < KD - 1:
                        link(ins)
                    else:
                        ins.then_inc(ada_acc_s, 1)
                if pending:
                    ada_finish()
                pending.append((n, s, col, bias))

            std = Tally()
            hh = Tally()

            def inverse(rs):
                ve.wait_ge(std_ready, std.next())
                link(V.reciprocal(rs, rs))

            cr = Tally()

            def model_inverse():
                ve.wait_ge(c_root, cr.next())
                V.reciprocal(rt[:, 0, 0:TT], rt[:, 0, 0:TT]).then_inc(c_inv, 1)
                ve.wait_ge(std_ready, std.next())

            def h_low(k, src):
                ve.wait_ge(h_hi, hh.next())
                V.tensor_tensor(hL[:, k, :], src, hH[:, k, :].bitcast(F32), ALU.subtract).then_inc(h_ready, 1)

            def modulated(g, sh, new=True):
                if new:
                    model_inverse()
                for k in range(KD + 1):
                    if k < KD:
                        b = k % 2
                        link(V.tensor_tensor(n_x[:, b, :], xT[:, k, :], n_rs[:, :], ALU.mult))
                        V.tensor_scalar(n_h[:, b, :], n_x[:, b, :], g[:, k:k + 1], sh[:, k:k + 1], ALU.mult, ALU.add)\
                            .then_inc(h_tmp, 1)
                    if k:
                        h_low(k - 1, n_h[:, (k - 1) % 2, :])

            def gains(dst, sc, g):
                link(V.scalar_tensor_tensor(dst, sc, 1.0, g, ALU.add, ALU.mult))

            V.memset(v_stage[:, :, :], 0.0).then_inc(vec_zero, 1)
            link(V.memset(small[:, :], 0.0))
            link(V.memset(small[64:96, 1:2], 1.0))
            link(V.memset(small[64:80, 1:2], -1.0))
            ve.wait_ge(vec_t, 1)
            V.tensor_copy(vec[:, :], PM[:, 2, 0:NVEC * P]).then_inc(vec_done, 1)
            for t in range(1, TT, 2):
                ve.wait_ge(x_t, t + 1)
                V.tensor_copy(xT[:, :, t * P:(t + 1) * P], PU[:, 1, :, :].rearrange("p a (b q) -> p (a b) q", q=P))\
                    .then_inc(x_ev[1], 1)
            ve.wait_ge(vec_done, 1)
            ve.wait_ge(cact_done, 1)

            def one(c):
                return slice(c, c + 1)

            def ada_bias():
                n = job.next()
                ve.wait_ge(ada_col, n)
                V.tensor_tensor(mod[:, n - 1:n], PM[:, 2 + (n - 1) % 2, 0:1], v("b_ada", n - 1), ALU.add).then_inc(ada_mod, 1)

            for j in range(16):
                ada_bias()
            ve.wait_ge(ada_mod, 16)
            link(V.tensor_scalar(small[:, 2:3], v("na_q_g"), HD ** -0.5, None, ALU.mult))
            gains(coef[:, 0, :], m("sc1", 0, 8), v("norm1_g", 0, 8))
            modulated(coef[:, 0, :], m("sh1", 0, 8))
            split()

            for n, (kind, t, c0) in enumerate(WIN_UNITS):
                split()
                for _ in range(ADA_AT_UNIT[n]):
                    ada_job(cact[:, 0:8], job.n, VEC["b_ada"][0] + job.n)
                if kind == "x":
                    skip()
                elif kind == "gc":
                    xp, xn = uc.at(-1)
                    ve.wait_ge(unit_free[xp], xn + 1)
                    if t == 0:
                        V.memset(conv_u[:, 0:1], 0.0)
                        link(V.memset(conv_u[:, T + 1:T + 2], 0.0))
                    p = unit()
                    free(V.tensor_tensor(conv_u[:, 1:T + 1], unit_ps(p), conv_x[:, :], ALU.mult))
                    ve.wait_ge(unit_free[p], uc.n // 2 if p else (uc.n + 1) // 2)
                elif kind == "gb":
                    link(V.tensor_scalar(conv_v[:, :], conv_u[:, 0:T], v("conv_w", t), v("conv_b", t), ALU.mult, ALU.add))
                    for tap in (1, 2):
                        link(V.scalar_tensor_tensor(conv_v[:, :], conv_u[:, tap:tap + T], v("conv_w", 2 * tap + t),
                                                    conv_v[:, :], ALU.mult, ALU.add))
                    p = unit()
                    free(V.tensor_tensor(y_conv[:, t, :], unit_ps(p), conv_v[:, :], ALU.mult))
                elif kind in ("q", "k"):
                    p = unit()
                    inverse(j_rs[:, :])
                    dst, g = (na_q, small[:, 2:3]) if kind == "q" else (na_k, v("na_k_g"))
                    free(V.scalar_tensor_tensor(dst[:, t, :], unit_ps(p), g, j_rs[:, :], ALU.mult, ALU.mult))
                elif kind == "v":
                    skip()
                elif kind in ("cq", "ckv"):
                    p, n_ = uc.at()
                    skip()
                    dst, tiles, g = (cq, 3, "q_a_g") if kind == "cq" else (ckv, 2, "kv_a_g")
                    if t == tiles - 1:
                        inverse(j_rs[:, :])
                        ve.wait_ge(unit_free[p], n_ + 1)
                        for k in range(tiles):
                            ins = V.scalar_tensor_tensor(dst[:, k, :], dst[:, k, :], v(g, k), j_rs[:, :], ALU.mult, ALU.mult)
                        ins.then_inc(j_done, 1)
                else:
                    skip()
                    inverse(j_rs[64:96, :])
                    V.scalar_tensor_tensor(k_raw[64:96, :], k_raw[64:96, :], v("mla_k_g", rows=ROPE, r0=64),
                                           j_rs[64:96, :], ALU.mult, ALU.mult).then_inc(j_done, 1)
            ada_finish()
            ve.wait_ge(ada_mod, 6 * KD)
            gains(coef[:, 1, :], m("sc2", 0, 8), v("norm2_g", 0, 8))

            NS = 16
            ve.wait_ge(b2_landed, 16 * 2 * NAH)
            for r0, s0 in ((0, 0), (64, 1)):
                for hh_ in range(NAH):
                    rows = b2[r0:r0 + 64, hh_, s0:s0 + 15, :]
                    ins = V.tensor_tensor(rows, rows, na_mask[r0:r0 + 64, :].unsqueeze(1).broadcast_to([64, 15, GRID]), ALU.add)
            link(ins)
            link(V.tensor_copy(bint[:, :, :, :], b2[:, :, 3:12, :]))
            V.memset(bint[0:64, :, 8, :], NEG)
            link(V.memset(bint[64:128, :, 0, :], NEG))
            with ve.Fori(0, NAH // 2) as i:
                ch.enter(i, 4 * NS)
                for j in range(NS + 2):
                    hp, pair = (j // 8) % 2, j % 8
                    b = j % 2
                    if j < NS:
                        if pair == 0:
                            V.tensor_copy(na_qs[:, hp, :], na_q[hp * 64:hp * 64 + 64, bass.ds(i, 1), :]
                                          .rearrange("p a b -> p (a b)")).then_inc(na_stage, 1)
                        wide = 2 <= pair <= 5
                        ve.wait_ge(na_s, i * NS + j + 1)
                        if j >= 2:
                            ve.wait_ge(na_tr, i * NS + j - 1)
                        hd = bass.ds(2 * i + hp, 1)
                        if wide:
                            src = unit_ps(b)[:, 0:576]
                            bias = bint[:, hd, :, :].rearrange("p h r w -> p (h r w)")
                        else:
                            src = PU[:, b, 0, :]
                            d0 = NA_PAIRS[pair][1]
                            bias = b2[:, hd, d0:d0 + 8, :].rearrange("p h r w -> p (h r w)")
                        w = 576 if wide else 512
                        link(V.tensor_tensor(na_p[:, b, 0:w], src, bias, ALU.add))
                        link(V.tensor_reduce(small[:, 12 + b:13 + b], na_p[:, b, 0:w], AX.X, ALU.max))
                        if j >= 2:
                            ve.wait_ge(na_e, i * NS + j - 1)
                        V.tensor_scalar(small[:, 8 + b:9 + b], small[:, 12 + b:13 + b], -1.0, None, ALU.mult)\
                            .then_inc(na_l, 1)
                    if j >= 2:
                        o_pair, o_hp = (j - 2) % 8, (j - 2) // 8
                        ve.wait_ge(na_e, i * NS + j - 1)
                        link(V.reciprocal(small[:, 14 + b:15 + b], small[:, 28 + (j - 2) % 4:29 + (j - 2) % 4]))
                        ve.wait_ge(na_pv, i * NS + j - 1)
                        V.tensor_scalar(y_na[:, o_pair, bass.ds((2 * i + o_hp) * HD, HD)], PM[:, 2 + b, 0:HD],
                                        small[:, 14 + b:15 + b], None, ALU.mult).then_inc(na_o, 1)
                        link(V.memset(small[:, 20:21], 0.0))
                ch.leave(NAH // 2)

            ve.wait_ge(rope_dma, 16)
            ve.wait_ge(rope_f, 16)
            R = slice(64, 96)
            posf, ang, tmp = rope[R, 0, :], rope_t[R, :], rope_k[R, :]
            link(V.tensor_copy(posf, rope_t[R, :].bitcast(I32)))
            link(V.tensor_scalar(ang, posf, kv_row[R, 0:1], None, ALU.mult))
            MAGIC = 1.5 * 2.0 ** 23
            for w, off in ((0, 0.25), (1, 0.0)):
                r = rope[R, w, :]
                link(V.tensor_scalar(tmp, ang, 1 / (2 * PI), off, ALU.mult, ALU.add))
                link(V.tensor_scalar(tmp, tmp, MAGIC, None, ALU.add))
                link(V.tensor_scalar(tmp, tmp, -MAGIC, None, ALU.add))
                link(V.scalar_tensor_tensor(r, tmp, -TWO_PI[0], ang, ALU.mult, ALU.add))
                link(V.scalar_tensor_tensor(r, tmp, -TWO_PI[1], r, ALU.mult, ALU.add))
                link(V.scalar_tensor_tensor(r, tmp, -TWO_PI[2], r, ALU.mult, ALU.add))
                if w == 0:
                    link(V.tensor_scalar(r, r, PI / 2, None, ALU.add))
                V.tensor_scalar(r, r, 3.1415925, -3.1415925, ALU.min, ALU.max).then_inc(rope_arg, 1)
            ve.wait_ge(rope_done, 2)
            link(V.tensor_scalar(rope[R, 1, :], rope[R, 1, :], small[R, 1:2], None, ALU.mult))
            swap = [(r + 16) % 32 for r in range(32)]

            def rotate(dst, src, last):
                link(V.stream_shuffle(rope_t[R, :], src, swap))
                link(V.tensor_tensor(rope_t[R, :], rope_t[R, :], rope[R, 1, :], ALU.mult))
                link(V.tensor_tensor(dst, src, rope[R, 0, :], ALU.mult))
                V.tensor_tensor(dst, dst, rope_t[R, :], ALU.add).then_inc(last, 1)

            rotate(rope_k[R, :], k_raw[R, :], rope_x)
            for n in range(2 * MH + 1):
                if n < 2 * MH:
                    ve.wait_ge(c_root, cr.next())
                    b = (n + 1) % 2
                    link(V.reciprocal(rt[:, b, 0:3 * TT], rt[:, b, 0:3 * TT]))
                    if n:
                        ve.wait_ge(c_bc, cr() - 1)
                    V.tensor_copy(inv3[:, :, :].rearrange("p t (g c) -> p (t g) c", c=32),
                                  rt[:, b, 0:3 * TT].unsqueeze(2).broadcast_to([P, 3 * TT, 32])).then_inc(c_inv, 1)
                if n:
                    hd = n - 1
                    rows = 96 if hd < MH else HD
                    dst = (mq if hd < MH else mk)[:, hd % MH, :]
                    gain = v("mla_q_g", rows=96) if hd < MH else v("mla_k_g", rows=HD)
                    ve.wait_ge(c_bc, cr() - (1 if n < 2 * MH else 0))
                    V.scalar_tensor_tensor(dst[0:rows, :], dst[0:rows, :], gain, stat_ps[0:rows, :], ALU.mult, ALU.mult)\
                        .then_inc(h_app, 1)
                    if hd < MH:
                        ve.wait_ge(h_app, hd + 1)
                        if hd:
                            ve.wait_ge(j_done, 3 + hd)
                        else:
                            ve.wait_ge(rope_x, 1)
                        rotate(dst[R, :], dst[R, :], j_done)
            skip(2 * MH)
            skip(TT // 2)
            for back in (1, 2):
                vp, vn = uc.at(-back)
                ve.wait_ge(unit_free[vp], vn + 1)

            scale = float(np.float32((HD + ROPE) ** -0.5))
            ve.wait_ge(j_done, 3 + MH)
            with ve.Fori(0, MH) as i:
                ch.enter(i, 3 * TT)
                for j in range(TT + 2):
                    b = j % 2
                    if j < TT:
                        if j >= 2:
                            ve.wait_ge(mla_s, i * TT + j - 1)
                        V.tensor_copy(m_qs[0:96, b, :], mq[0:96, bass.ds(i, 1), j * P:(j + 1) * P]
                                      .rearrange("p a b -> p (a b)")).then_inc(mla_q, 1)
                        ve.wait_ge(mla_s, i * TT + j + 1)
                        link(V.tensor_reduce(small[:, 22 + b:23 + b], unit_ps(b), AX.X, ALU.max))
                        if j >= 2:
                            ve.wait_ge(mla_e, i * TT + j - 1)
                        V.tensor_scalar(small[:, 16 + b:17 + b], small[:, 22 + b:23 + b], -scale, None, ALU.mult)\
                            .then_inc(mla_m, 1)
                    if j >= 2:
                        ve.wait_ge(mla_e, i * TT + j - 1)
                        link(V.reciprocal(small[:, 24 + b:25 + b], small[:, 32 + (j - 2) % 4:33 + (j - 2) % 4]))
                        ve.wait_ge(mla_pv, i * TT + j - 1)
                        V.tensor_scalar(y_mla[:, j - 2, bass.ds(i * HD, HD)], PM[:, 2 + b, 0:HD],
                                        small[:, 24 + b:25 + b], None, ALU.mult).then_inc(mla_o, 1)
                        link(V.memset(small[:, 21:22], 0.0))
                ch.leave(MH)

            for t in range(2):
                inverse(u_rs[:, :])
                V.scalar_tensor_tensor(g_h[:, t, :], y_conv[:, t, :], v("out_norm_g", 6 + t), u_rs[:, :], ALU.mult, ALU.mult)\
                    .then_inc(h_tmp, 1)
                h_low(6 + t, g_h[:, t, :])
            for w, (y, n, c0) in enumerate(((y_na, 32, 0), (y_mla, 64, 32))):
                yg = y[:, :, :].rearrange("p t (g c) -> p (t g) c", c=HD)
                ve.wait_ge(y_sq, w + 1)
                V.tensor_reduce(g_rs[:, c0:c0 + n], g_sq[:, 0:n * HD].rearrange("p (g c) -> p g c", c=HD), AX.X, ALU.add)\
                    .then_inc(y_sum, 1)
                ve.wait_ge(y_root, w + 1)
                link(V.reciprocal(g_rs[:, c0:c0 + n], g_rs[:, c0:c0 + n]))
                V.tensor_tensor(yg, yg, g_rs[:, c0:c0 + n].unsqueeze(2).broadcast_to([P, n, HD]), ALU.mult).then_inc(y_norm, 1)
            for f in range(7):
                if f < 6:
                    p = unit()
                    ve.wait_ge(h_ready, hh())
                    free(V.tensor_scalar(g_h[:, f % 2, :], unit_ps(p), v("out_norm_g", f), None, ALU.mult))
                if f:
                    h_low(f - 1, g_h[:, (f - 1) % 2, :])
            for t in range(KD):
                split()
                p = unit()
                free(V.scalar_tensor_tensor(xT[:, t, :], unit_ps(p), m("g1", t), xT[:, t, :], ALU.mult, ALU.add))

            modulated(coef[:, 1, :], m("sh2", 0, 8))

            def gate(jobs=()):
                split()
                for args in jobs:
                    ada_job(cact[:, 8:16], *args)
                skip()

            fh = Tally()

            def up(t, jobs=()):
                gp, gn = uc.at(-1)
                split()
                for args in jobs:
                    ada_job(cact[:, 8:16], *args)
                p = unit()
                ve.wait_ge(unit_free[gp], gn + 1)
                if fh.n:
                    ve.wait_ge(f_act, fh())
                free(V.tensor_tensor(f_prod[:, t, :], unit_ps(p), f_silu[:, t, :], ALU.mult))

            def low(t):
                ve.wait_ge(f_hi_s, fh.next())
                V.tensor_tensor(f_lo[:, t, :], f_prod[:, t, :], f_hi[:, t, :].bitcast(F32), ALU.subtract).then_inc(f_act, 1)

            def down_units(g, tiles):
                split()
                for t in tiles:
                    p = unit()
                    free(V.scalar_tensor_tensor(xT[:, t, :], unit_ps(p), m(g, t), xT[:, t, :], ALU.mult, ALU.add))

            def ffn_body(i, times, jobs):
                for c, per in ((pc, 6), (uc, 12), (fh, 2), (job, jobs), (ch, (KD - 1) * jobs)):
                    c.enter(i, per)
                todo = []
                if jobs:
                    for l in range(2):
                        for j in range(3):
                            c = 48 + 24 * l + j + 3 * i
                            todo.append((c, c + 80))
                    for j in range(2):
                        c = 96 + j + 2 * i
                        todo.append((c, c + 80))
                gate(todo[0:2])
                up(0, todo[2:4])
                gate(todo[4:6])
                down_units("g2", range(4))
                down_units("g2", range(4, 8))
                low(0)
                up(1, todo[6:8])
                low(1)
                if jobs:
                    ada_finish()
                for c in (pc, uc, fh, job, ch):
                    c.leave(times)

            for t in range(2):
                gate()
                up(t)
                low(t)
            with ve.Fori(0, 8) as i:
                ffn_body(i, 8, 8)
            with ve.Fori(0, FT // 2 - 9) as i:
                ffn_body(i, FT // 2 - 9, 0)
            down_units("g2", range(4))
            down_units("g2", range(4, 8))

            gains(coef[:, 2, :], m("m_sc", 0, 8), v("norm_g_2", 0, 8))
            gains(coef[:, 3, :], m("kv_sc", 0, 8), v("kv_norm_g_2", 0, 8))
            gains(coef[:, 4, :], m("s_sc", 0, 8), v("norm_g_2", 8, 8))
            modulated(coef[:, 2, :], m("m_sh", 0, 8))
            split()
            W = [dt_w[:, k, :] for k in range(4)]
            p = unit()
            free(V.tensor_scalar(W[0], unit_ps(p, NH), v("dt_bias", rows=NH), None, ALU.add))
            ve.wait_ge(unit_free[p], (uc.n - 1) // 2 + 1)
            V.scalar_tensor_tensor(W[1], W[0], -1.0, W[0], ALU.mult, ALU.min).then_inc(dt_x, 1)
            ve.wait_ge(dt_x, 2)
            link(V.tensor_scalar(W[2], W[1], 2.0, None, ALU.add))
            link(V.reciprocal(W[2], W[2]))
            link(V.tensor_tensor(W[1], W[1], W[2], ALU.mult))
            link(V.tensor_tensor(W[2], W[1], W[1], ALU.mult))
            link(V.tensor_scalar(W[3], W[2], 2 / 13, None, ALU.mult))
            for odd in (11, 9, 7, 5, 3):
                link(V.scalar_tensor_tensor(W[3], W[3], 2 / odd, W[2], ALU.add, ALU.mult))
            link(V.scalar_tensor_tensor(W[3], W[3], 2.0, W[1], ALU.add, ALU.mult))
            link(V.scalar_tensor_tensor(W[2], W[0], 0.0, W[3], ALU.max, ALU.add))
            V.tensor_scalar(W[3], W[2], small[0:NH, 40:41], -1.0, ALU.mult, ALU.mult).then_inc(dt_f, 1)
            ve.wait_ge(dt_t_s, 1)
            V.tensor_copy(dt_t[:, :, :].rearrange("p a b -> p (a b)"), PM[:, 0, 0:256])
            V.tensor_copy(a_t[:, :, :].rearrange("p a b -> p (a b)"), PM[:, 1, 0:256]).then_inc(dt_tok, 1)
            ve.wait_ge(dt_sum, 1)
            link(V.tensor_copy(acum[:, :, :].rearrange("p a b -> p (a b)"), PM[:, 2, 0:256]))
            link(V.tensor_copy(etot[:, :, :].rearrange("p a b -> p (a b)"), PM[:, 2, 256:512]))
            V.tensor_tensor(wend[:, :, :], etot[:, :, :], acum[:, :, :], ALU.subtract).then_inc(dt_log, 1)
            ve.wait_ge(dt_exp, 1)
            V.tensor_tensor(wend[:, :, :], wend[:, :, :], dt_t[:, :, :], ALU.mult).then_inc(dt_done, 1)
            ve.wait_ge(dt_done, 1)
            ve.wait_ge(d_landed, 16)

            c_w = vec[:, VEC["m_conv_w_2"][0]:VEC["m_conv_w_2"][0] + 96].rearrange("p (k c) -> p k c", k=4)
            c_b, n_g = VEC["m_conv_b_2"][0], VEC["m_norm_g_2"][0]
            with counted(ve, NG, [(pc, 14), (uc, 22), (ch, 51)]) as i:
                for dst, n, c0 in ((0, 4, 4 * i), (4, 1, 16 + i), (5, 1, 20 + i)):
                    V.tensor_copy(cg_w[:, :, dst:dst + n], c_w[:, :, bass.ds(c0, n)])
                    link(V.tensor_copy(cg_b[:, dst:dst + n], vec[:, bass.ds(c_b + c0, n)]))
                V.tensor_copy(ng[:, 0:4], vec[:, bass.ds(n_g + 4 * i, 4)])
                for k, row in enumerate((dt_t, wend)):
                    V.tensor_copy(pool_t[:, k, :].rearrange("p (c h) -> p c h", h=8), row[:, :, bass.ds(8 * i, 8)])
                V.tensor_copy(pool_t[:, 2, :].rearrange("p (c h) -> p c h", h=8),
                              d_row[:, bass.ds(8 * i, 8)].unsqueeze(1).broadcast_to([P, TT, 8]))
                V.tensor_copy(acg[:, :, :], acum[:, :, bass.ds(8 * i, 8)])
                V.tensor_copy(ag[:, :, :], a_t[:, :, bass.ds(8 * i, 8)]).then_inc(ag_done, 1)
                V.memset(c_raw[:, 0, 0:3], 0.0)
                link(V.memset(c_raw[:, 1, 0:3], 0.0))
                for j in range(6):
                    split()
                    p, n = uc.at()
                    skip()
                    ve.wait_ge(unit_free[p], n + 1)
                    if j >= 2:
                        ve.wait_ge(cv_tr, 9 * i + j - 1)
                    raw, o = c_raw[:, j % 2, :], c_out[:, j % 2, :]
                    link(V.tensor_scalar(o, raw[:, 0:T], cg_w[:, 0, j:j + 1], cg_b[:, j:j + 1], ALU.mult, ALU.add))
                    for tap in (1, 2, 3):
                        ins = V.scalar_tensor_tensor(o, raw[:, tap:tap + T], cg_w[:, tap, j:j + 1], o, ALU.mult, ALU.add)
                        if tap < 3:
                            link(ins)
                        else:
                            ins.then_inc(cv_done, 1)
                for j in range(4):
                    split()
                    skip()
                ve.wait_ge(cv_tok, 9 * i + 9)
                for j in range(TT + 1):
                    b = j % 2
                    if j < TT:
                        ve.wait_ge(ss_bc, TT * i + j + 1)
                        if j >= 2:
                            ve.wait_ge(ss_y, TT * i + j - 1)
                        V.tensor_tensor(seg[:, b, :, :], PU[:, 0, :, :].rearrange("p a (h t) -> p (a h) t", t=P),
                                        acg[:, j, :].unsqueeze(2).broadcast_to([P, 8, P]), ALU.subtract).then_inc(ss_seg, 1)
                        V.tensor_tensor(cbm[:, b, :], PU[:, 1, 1, 0:P], tri[:, :], ALU.mult).then_inc(ss_cbr, 1)
                    if j < TT - 1:
                        ve.wait_ge(ss_s, (TT - 1) * i + j + 1)
                        if j == 0:
                            V.tensor_copy(state[:, 0, :], PU[:, 1, 0, :]).then_inc(ss_st, 1)
                        else:
                            if j >= 2:
                                ve.wait_ge(ss_off, (TT - 1) * i + j - 1)
                            ve.wait_ge(ss_st, (TT - 1) * i + j)
                            link(V.tensor_tensor(state[:, b, :].rearrange("p (h d) -> p h d", h=8),
                                                 state[:, 1 - b, :].rearrange("p (h d) -> p h d", h=8),
                                                 etot[:, j, bass.ds(8 * i, 8)].unsqueeze(2).broadcast_to([P, 8, HD]), ALU.mult))
                            V.tensor_tensor(state[:, b, :], state[:, b, :], PU[:, 1, 0, :], ALU.add).then_inc(ss_st, 1)
                    if j:
                        c, b1 = j - 1, (j - 1) % 2
                        ve.wait_ge(ss_y, TT * i + c + 1)
                        if c:
                            ve.wait_ge(ss_g, TT * i + c)
                        if c:
                            link(V.tensor_tensor(y1[:, :].rearrange("p (h d) -> p h d", h=8),
                                                 PM[:, 2 + b1, :].rearrange("p (h d) -> p h d", h=8),
                                                 eacum[:, c, bass.ds(8 * i, 8)].unsqueeze(2).broadcast_to([P, 8, HD]), ALU.mult))
                            link(V.tensor_tensor(y1[:, :], y1[:, :], PM[:, b1, :], ALU.add))
                        ve.wait_ge(ss_x, (3 * TT - 1) * i + (3 * c + 3 if c < TT - 1 else 3 * TT - 1))
                        link(V.tensor_tensor(y1[:, :], y1[:, :] if c else PM[:, b1, :], xd[:, b1, :], ALU.add))
                        V.tensor_tensor(zt[:, c, :], zt[:, c, :], y1[:, :], ALU.mult).then_inc(ss_g, 1)
                    if j < TT:
                        ve.wait_ge(ss_exp, TT * i + j + 1)
                        ve.wait_ge(ss_cbr, TT * i + j + 1)
                        V.tensor_tensor(seg[:, b, :, :], seg[:, b, :, :],
                                        cbm[:, b, :].unsqueeze(1).broadcast_to([P, 8, P]), ALU.mult).then_inc(ss_m, 1)
                ve.wait_ge(m_root, i + 1)
                link(V.reciprocal(m_ss[:, :], m_ss[:, :]))
                V.tensor_tensor(zt[:, :, :], zt[:, :, :], m_ss[:, :].unsqueeze(2).broadcast_to([P, TT, 512]), ALU.mult)\
                    .then_inc(m_norm, 1)
                for f in range(5):
                    if f < 4:
                        p, n = uc.at()
                        unit()
                        if f >= 2:
                            ve.wait_ge(y_lo_s, 4 * i + f - 1)
                        free(V.tensor_scalar(y_t32[:, f % 2, :], unit_ps(p), ng[:, f:f + 1], None, ALU.mult))
                    if f:
                        ve.wait_ge(y_hi_s, 4 * i + f)
                        V.tensor_tensor(y_lo[:, f - 1, :], y_t32[:, (f - 1) % 2, :], y_hi[:, f - 1, :].bitcast(F32), ALU.subtract)\
                            .then_inc(y_lo_s, 1)
                for c in range(4):
                    down_units("m_g", (2 * c, 2 * c + 1))
            for w in range(2):
                if w:
                    V.memset(small[:, 41:42], 0.0).then_inc(o_mask, 1)
                modulated(coef[:, 3 + w, :], m("s_sh" if w else "kv_sh", 0, 8), new=w == 0)
                if w == 0:
                    V.memset(small[:, 42:43], 0.0).then_inc(v_ev, 1)
                with counted(ve, KD, [(pc, 2), (uc, 2)]) as i:
                    split()
                    if w == 0:
                        skip()
                        split()
                    p = unit()
                    free(V.tensor_copy(stage[:, 2 * w, :], unit_ps(p)))
                    if w == 0:
                        ve.wait_ge(v_tr, i + 1)
                        V.tensor_copy(stage[:, 1, :], stat_ps).then_inc(v_ev, 1)
                        ve.wait_ge(st_done[1], 16 * (i + 1))
                    else:
                        split()
                        skip()
                    ve.wait_ge(st_done[2 * w], 16 * (i + 1))
                if w == 0:
                    lp, ln = uc.at(-1)
                    ve.wait_ge(unit_done[lp], ln + 1)
            NS = 32
            with counted(ve, SBH // 4, [(ch, NS)]) as i:
                for j in range(1, NS + 3):
                    if j <= NS:
                        n = j - 1
                        w = (n % 8 + 1) * P
                        ve.wait_ge(s_mk, NS * i + n + 1)
                        if n:
                            ve.wait_ge(s_a, NS * i + n)
                        link(V.tensor_tensor_scan(s_prod[:, 0:w][:, ::-1], s_keep[:, n % 2, 0:w][:, ::-1],
                                                  later[:, T - w:T][:, ::-1], 1.0, ALU.mult, ALU.max))
                        sg = s_sig[:, n % 3, 0:w - 1]
                        V.tensor_tensor(sg, sg, s_prod[:, 1:w], ALU.mult).then_inc(s_a, 1)
                    if j >= 3:
                        n = j - 3
                        pb, hd, qt = n // 16, (n // 8) % 2, n % 8
                        ve.wait_ge(s_pv, NS * i + n + 1)
                        r = slice(hd * HD, (hd + 1) * HD)
                        V.tensor_tensor(s_of[r, pb, qt * P:(qt + 1) * P], PM[r, 2 + n % 2, 0:P],
                                        s_z[r, pb, qt * P:(qt + 1) * P], ALU.mult).then_inc(s_o, 1)
                    if j in (20, NS + 2):
                        pb = j // 32
                        ve.wait_ge(ep_hi, 2 * i + pb + 1)
                        V.tensor_tensor(hL[:, bass.ds(2 * i + pb, 1), :].rearrange("p a b -> p (a b)"), s_of[:, pb, :],
                                        hH[:, bass.ds(2 * i + pb, 1), :].rearrange("p a b -> p (a b)").bitcast(F32),
                                        ALU.subtract).then_inc(ep_lo, 1)
                    n = j - 2
                    if 0 <= n < NS and n % 2 == 0:
                        ve.wait_ge(s_tr, NS * i + n + 1)
                        if n >= 2:
                            ve.wait_ge(s_pv, NS * i + n - 1)
                        w = (n % 8 + 1) * P
                        V.tensor_copy(s_at[:, 0, :, :].rearrange("p a b -> p (a b)")[:, 0:w], stat_ps[:, 0:w])\
                            .then_inc(s_ev[0], 1)
            for t in range(KD):
                if t < KD - 1:
                    split()
                p = unit()
                free(V.scalar_tensor_tensor(xT[:, t, :], unit_ps(p), m("s_g", t), xT[:, t, :], ALU.mult, ALU.add))
            model_inverse()
            for k in range(KD):
                if k >= 2:
                    lp, ln = uc.at(k - 2)
                    ve.wait_ge(unit_done[lp], ln + 1)
                V.scalar_tensor_tensor(n_x[:, k % 2, :], xT[:, k, :], v("final_g_2", k), n_rs[:, :], ALU.mult, ALU.mult)\
                    .then_inc(o_xn, 1)



N_VEC_DMA = 28


def VEC_ROWS(a):
    def rows(x):
        return x.rearrange("o (r c) -> (o r) c", c=P)

    yield "norm1_g", rows(a["norm1_g"]), 8, P
    yield "norm2_g", rows(a["norm2_g"]), 8, P
    yield "b_ada", rows(a["b_ada"]), 48, P
    yield "conv_w", a["conv_w"].rearrange("o k (r c) -> (o k r) c", c=P), 6, P
    yield "conv_b", rows(a["conv_b"]), 2, P
    yield "q_a_g", rows(a["mla_q_a_g"]), 3, P
    yield "kv_a_g", rows(a["mla_kv_a_g"]), 2, P
    yield "out_norm_g", rows(a["out_norm_g"]), 8, P
    yield "ada_b_2", rows(a["ada_b_2"]), 48, P
    yield "kv_ada_b_2", a["kv_ada_b_2"].rearrange("(r c) -> r c", c=P), 16, P
    yield "norm_g_2", rows(a["norm_g_2"]), 16, P
    yield "m_conv_b_2", rows(a["m_conv_b_2"]), 24, P
    yield "kv_norm_g_2", a["kv_norm_g_2"].rearrange("(r c) -> r c", c=P), 8, P
    yield "final_g_2", a["final_g_2"].rearrange("(r c) -> r c", c=P), 8, P
    yield "m_conv_w_2", a["m_conv_w_2"].rearrange("o k (r c) -> (o k r) c", c=P), 96, P
    yield "m_norm_g_2", rows(a["m_norm_g_2"]), 16, P
    yield "c", rows(a["c"]), 8, P
    yield "c_2", rows(a["c_2"]), 8, P
    yield "dt_bias", a["m_dt_bias_2"], 1, NH
    yield "a_log", a["m_a_log_2"], 1, NH


def VEC_PARTS(a):
    for off in (0, HD):
        yield "na_q_g", a["na_q_g"], off, HD
        yield "na_k_g", a["na_k_g"], off, HD
    yield "mla_q_g", a["mla_qn_g"], 0, HD
    yield "mla_q_g", a["mla_qr_g"], HD, ROPE
    yield "mla_k_g", a["mla_kn_g"], 0, HD
    yield "mla_k_g", a["mla_kr_g"], HD, ROPE


_INS = ["x", "c", "positions", "norm1_g", "norm2_g", "w_ada", "b_ada", "w_in", "na_q_g", "na_k_g", "na_rpb",
        "mla_q_a_g", "mla_kv_a_g", "mla_w_uq", "mla_w_ukv", "mla_qn_g", "mla_kn_g", "mla_qr_g", "mla_kr_g",
        "conv_w", "conv_b", "out_norm_g", "w_out", "w_gu", "w_down", "c_2", "ada_w_2", "ada_b_2", "norm_g_2",
        "m_in_w_2", "m_conv_w_2", "m_conv_b_2", "m_dt_bias_2", "m_a_log_2", "m_d_2", "m_norm_g_2", "m_out_w_2",
        "kv_ada_w_2", "kv_ada_b_2", "kv_norm_g_2", "kv_w_2", "sb_in_w_2", "sb_out_w_2", "final_g_2"]


def build(nc, arrays, debug=()):
    aps = {}
    for name, arr in arrays.items():
        aps[name] = nc.dram_tensor(f"in_{name}_dram", arr.shape, mybir.dt.from_np(arr.dtype), kind="ExternalInput").ap()
    out = nc.dram_tensor("out_0_dram", (1, T, D), F32, kind="ExternalOutput").ap()
    for name, shape in debug:
        aps["dbg_" + name] = nc.dram_tensor("dbg_" + name, shape, F32, kind="ExternalOutput").ap()
    two_blocks(nc, aps, out)


def kernel(**inputs):
    import concourse.bacc as bacc
    from concourse.bass_utils import run_bass_kernel_spmd

    nc = bacc.Bacc("TRN2", target_bir_lowering=False, num_devices=1)
    arrays = {name: np.ascontiguousarray(inputs[name]) for name in _INS}
    inv = (np.float32(10000.0) ** (-np.arange(0, ROPE, 2, dtype=np.float32) / np.float32(ROPE))).astype(np.float32)
    arrays["rope_inv"] = np.concatenate([inv, inv]).reshape(ROPE, 1)
    build(nc, arrays)
    r = run_bass_kernel_spmd(nc, [{f"in_{n}_dram": arr for n, arr in arrays.items()}], core_ids=[0])
    return np.asarray(r.results[0]["out_0_dram"])
```
